# Optimizing a Trainium2 kernel written in Bass

```python
import jax, jax.numpy as jnp
from jax import lax
import numpy as np

D_MODEL = 1024
BATCH = 1
SEQ = 512
DEPTH = 2

CHUNK = 64
EPS = 1e-6
PLE_DIM = 256
D_FF = 2816
FFN_RES = 0.5
N_EVEN = (DEPTH + 1) // 2
N_ODD = DEPTH // 2

GLA_HEADS = 4
GLA_V = D_MODEL // 2
GLA_DV = GLA_V // GLA_HEADS
GLA_QK = GLA_V // 2
GLA_DK = GLA_QK // GLA_HEADS
GLA_RANK = 16
GLA_GATE_TEMP = 16.0

LRU_WIDTH = D_MODEL // 2
LRU_BLOCKS = 8
LRU_BW = LRU_WIDTH // LRU_BLOCKS
CONV_W = 4
LRU_C = 8.0

MIX0_SPLITS = [int(c) for c in np.cumsum([GLA_QK, GLA_QK, GLA_V, GLA_V, GLA_RANK, LRU_WIDTH])]
MIX0_COLS = 2 * GLA_QK + 2 * GLA_V + GLA_RANK + 2 * LRU_WIDTH
MIX0_OUT = GLA_V + LRU_WIDTH

HG_DK = 128
HG_HEADS = D_MODEL // HG_DK
HG_DV = 128
HG_K = HG_HEADS * HG_DK
HG_V = HG_HEADS * HG_DV
MIX1_SPLITS = [HG_K, 2 * HG_K, 2 * HG_K + HG_V]
MIX1_COLS = 2 * HG_K + 2 * HG_V


def rmsnorm(x, g):
    xf = x.astype(jnp.float32)
    y = xf * lax.rsqrt(jnp.mean(xf * xf, axis=-1, keepdims=True) + EPS)
    return (y * g.astype(jnp.float32)).astype(x.dtype)

def swiglu(h, w1, w3, w2):
    return (jax.nn.silu(h @ w1) * (h @ w3)) @ w2

def chunk_end_gated_linear_attention(q, k, v, log_f):
    b, s, h, dk = q.shape
    dv = v.shape[-1]
    n = s // CHUNK

    def chunks(t):
        return jnp.moveaxis(t.astype(jnp.float32).reshape(b, n, CHUNK, h, t.shape[-1]), 1, 0)

    qc, kc, vc, lf = chunks(q), chunks(k), chunks(v), chunks(log_f)
    cum = jnp.cumsum(lf, axis=2)
    total = cum[:, :, -1]
    k_dec = kc * jnp.exp(total[:, :, None] - cum)
    g_chunk = jnp.exp(total)

    def step(state, xs):
        q_c, k_c, v_c, g_c = xs
        state = g_c[..., None] * state + jnp.einsum('bchk,bchv->bhkv', k_c, v_c)
        return state, jnp.einsum('bchk,bhkv->bchv', q_c, state)

    s0 = jnp.zeros((b, h, dk, dv), jnp.float32)
    _, o = lax.scan(step, s0, (qc, k_dec, vc, g_chunk))
    return jnp.moveaxis(o, 0, 1).reshape(b, s, h, dv).astype(v.dtype)

def causal_depthwise_conv(x, w, bias):
    s = x.shape[1]
    xp = jnp.pad(x, ((0, 0), (CONV_W - 1, 0), (0, 0)))
    out = xp[:, 0:s] * w[0]
    for j in range(1, CONV_W):
        out = out + xp[:, j:j + s] * w[j]
    return out + bias

def block_diag(x, w, bias):
    b, s, wd = x.shape
    xb = x.reshape(b, s, LRU_BLOCKS, LRU_BW)
    return jnp.einsum('bsgi,gij->bsgj', xb, w).reshape(b, s, wd) + bias

def rg_lru(x, w_a, b_a, w_x, b_x, lam):
    r = jax.nn.sigmoid(block_diag(x, w_a, b_a)).astype(jnp.float32)
    i = jax.nn.sigmoid(block_diag(x, w_x, b_x))
    log_a = LRU_C * r * jax.nn.log_sigmoid(lam.astype(jnp.float32))
    a = jnp.exp(log_a)
    u = jnp.sqrt(-jnp.expm1(2.0 * log_a)) * (i * x).astype(jnp.float32)

    def combine(left, right):
        a1, b1 = left
        a2, b2 = right
        return a1 * a2, a2 * b1 + b2

    _, hs = lax.associative_scan(combine, (a, u), axis=1)
    return hs.astype(x.dtype)

def mixer_gla_rglru(h, w_in, gla_gate_up, gla_gate_bias, gla_head_norm, conv_w, conv_b,
                    lru_wa, lru_ba, lru_wx, lru_bx, lru_lambda, w_out):
    b, s, _ = h.shape
    z = h @ w_in
    q, k, v, g, lr, xr, xg = jnp.split(z, MIX0_SPLITS, axis=-1)
    log_f = jax.nn.log_sigmoid((lr @ gla_gate_up + gla_gate_bias).astype(jnp.float32)) / GLA_GATE_TEMP
    o = chunk_end_gated_linear_attention(
        q.reshape(b, s, GLA_HEADS, GLA_DK) * (GLA_DK ** -0.5),
        k.reshape(b, s, GLA_HEADS, GLA_DK),
        v.reshape(b, s, GLA_HEADS, GLA_DV),
        log_f.reshape(b, s, GLA_HEADS, GLA_DK))
    o = rmsnorm(o, gla_head_norm).reshape(b, s, GLA_V) * jax.nn.silu(g)
    y = rg_lru(causal_depthwise_conv(xr, conv_w, conv_b), lru_wa, lru_ba, lru_wx, lru_bx, lru_lambda)
    y = y * jax.nn.gelu(xg)
    return jnp.concatenate([o, y], axis=-1) @ w_out

def mixer_hgrn2(h, w_in, lb, hg_head_norm, w_out):
    b, s, _ = h.shape
    z = h @ w_in
    q, fz, i, g = jnp.split(z, MIX1_SPLITS, axis=-1)
    lbf = lb.astype(jnp.float32)
    zf = fz.astype(jnp.float32)
    log_f = jnp.logaddexp(jnp.log(lbf), jnp.log1p(-lbf) + jax.nn.log_sigmoid(zf))
    k = (1.0 - lbf) * jax.nn.sigmoid(-zf)
    o = chunk_end_gated_linear_attention(
        jax.nn.silu(q).reshape(b, s, HG_HEADS, HG_DK),
        k.astype(h.dtype).reshape(b, s, HG_HEADS, HG_DK),
        i.reshape(b, s, HG_HEADS, HG_DV),
        log_f.reshape(b, s, HG_HEADS, HG_DK))
    o = rmsnorm(o, hg_head_norm).reshape(b, s, HG_V) * jax.nn.silu(g)
    return o @ w_out

def lower_bounds(lb_logits):
    sm = jax.nn.softmax(lb_logits.astype(jnp.float32), axis=0)
    return jnp.cumsum(sm, axis=0) - sm[0]

def half_ffn(x, g, w1, w3, w2):
    return x + FFN_RES * swiglu(rmsnorm(x, g), w1, w3, w2)

def first_inputs(seed: int = 0) -> dict:
    key = jax.random.key(seed)
    ks = iter(list(jax.random.split(key, 40)))

    def nrm(shape, scale):
        return jax.random.normal(next(ks), shape, jnp.float32) * scale

    def gain(shape):
        return 1.0 + nrm(shape, 0.05)

    a0 = jax.random.uniform(next(ks), (N_EVEN, LRU_WIDTH), jnp.float32, 0.9, 0.999)
    return {
        'x': nrm((BATCH, SEQ, D_MODEL), 1.0),
        'p': nrm((DEPTH, BATCH, SEQ, PLE_DIM), 1.0),
        'ffn_norm': gain((DEPTH, 2, D_MODEL)),
        'ffn_w1': nrm((DEPTH, 2, D_MODEL, D_FF), D_MODEL ** -0.5),
        'ffn_w3': nrm((DEPTH, 2, D_MODEL, D_FF), D_MODEL ** -0.5),
        'ffn_w2': nrm((DEPTH, 2, D_FF, D_MODEL), D_FF ** -0.5),
        'mix_norm': gain((DEPTH, D_MODEL)),
        'ple_norm': gain((DEPTH, D_MODEL)),
        'ple_proj': nrm((DEPTH, PLE_DIM, D_MODEL), PLE_DIM ** -0.5),
        'ple_gate': nrm((DEPTH, D_MODEL, D_MODEL), D_MODEL ** -0.5),
        'final_norm': gain((D_MODEL,)),
        'm0_w_in': nrm((N_EVEN, D_MODEL, MIX0_COLS), D_MODEL ** -0.5),
        'gla_gate_up': nrm((N_EVEN, GLA_RANK, GLA_QK), GLA_RANK ** -0.5),
        'gla_gate_bias': nrm((N_EVEN, GLA_QK), 0.1),
        'gla_head_norm': gain((N_EVEN, GLA_DV)),
        'lru_conv_w': nrm((N_EVEN, CONV_W, LRU_WIDTH), CONV_W ** -0.5),
        'lru_conv_b': nrm((N_EVEN, LRU_WIDTH), 0.02),
        'lru_wa': nrm((N_EVEN, LRU_BLOCKS, LRU_BW, LRU_BW), LRU_BW ** -0.5),
        'lru_ba': nrm((N_EVEN, LRU_WIDTH), 0.02),
        'lru_wx': nrm((N_EVEN, LRU_BLOCKS, LRU_BW, LRU_BW), LRU_BW ** -0.5),
        'lru_bx': nrm((N_EVEN, LRU_WIDTH), 0.02),
        'lru_lambda': jnp.log(a0) - jnp.log1p(-a0),
        'm0_w_out': nrm((N_EVEN, MIX0_OUT, D_MODEL), MIX0_OUT ** -0.5),
        'm1_w_in': nrm((N_ODD, D_MODEL, MIX1_COLS), D_MODEL ** -0.5),
        'hgrn_lb_logits': nrm((DEPTH, HG_K), 0.1),
        'hgrn_head_norm': gain((N_ODD, HG_DV)),
        'm1_w_out': nrm((N_ODD, HG_V, D_MODEL), HG_V ** -0.5),
    }

def first_block(x, p, ffn_norm, ffn_w1, ffn_w3, ffn_w2, mix_norm, ple_norm, ple_proj, ple_gate,
              final_norm, m0_w_in, gla_gate_up, gla_gate_bias, gla_head_norm, lru_conv_w,
              lru_conv_b, lru_wa, lru_ba, lru_wx, lru_bx, lru_lambda, m0_w_out, m1_w_in,
              hgrn_lb_logits, hgrn_head_norm, m1_w_out):
    lbs = lower_bounds(hgrn_lb_logits)
    for layer in range(DEPTH):
        x = half_ffn(x, ffn_norm[layer, 0], ffn_w1[layer, 0], ffn_w3[layer, 0], ffn_w2[layer, 0])
        h = rmsnorm(x, mix_norm[layer])
        if layer % 2 == 0:
            e = layer // 2
            x = x + mixer_gla_rglru(h, m0_w_in[e], gla_gate_up[e], gla_gate_bias[e], gla_head_norm[e],
                                    lru_conv_w[e], lru_conv_b[e], lru_wa[e], lru_ba[e], lru_wx[e],
                                    lru_bx[e], lru_lambda[e], m0_w_out[e])
        else:
            o = layer // 2
            x = x + mixer_hgrn2(h, m1_w_in[o], lbs[layer], hgrn_head_norm[o], m1_w_out[o])
        x = half_ffn(x, ffn_norm[layer, 1], ffn_w1[layer, 1], ffn_w3[layer, 1], ffn_w2[layer, 1])
        gate = jax.nn.sigmoid(rmsnorm(x, ple_norm[layer]) @ ple_gate[layer])
        x = x + gate * (p[layer] @ ple_proj[layer])
    return rmsnorm(x, final_norm)


MLA_HEADS = 8
QK_NOPE_DIM = 64
QK_ROPE_DIM = 32
V_HEAD_DIM = 64
Q_LORA_RANK = 256
KV_LORA_RANK = 128
QK_HEAD_DIM = QK_NOPE_DIM + QK_ROPE_DIM
D_ATTN = MLA_HEADS * V_HEAD_DIM
ROPE_THETA = 10000.0
Q_BLOCK = 128
SSD_HEADS = 8
SSD_HEAD_DIM = 64
SSD_GROUPS = 2
SSD_STATE = 128
CONV_WIDTH = 4
CHUNK_2 = 128
D_SSD = SSD_HEADS * SSD_HEAD_DIM
D_CONV = D_SSD + 2 * SSD_GROUPS * SSD_STATE
D_MIX = D_ATTN + D_SSD
D_IN = Q_LORA_RANK + KV_LORA_RANK + QK_ROPE_DIM + D_SSD + D_CONV + SSD_HEADS
D_FF_2 = ((-(-8 * D_MODEL // 3) + 255) // 256) * 256
N_MOD = 6


def rmsnorm_2(x, w):
    xf = x.astype(jnp.float32)
    y = xf * lax.rsqrt(jnp.mean(xf * xf, axis=-1, keepdims=True) + EPS)
    return (y * w.astype(jnp.float32)).astype(x.dtype)

def rope(x, cos, sin):
    x1, x2 = jnp.split(x, 2, axis=-1)
    return jnp.concatenate([x1 * cos - x2 * sin, x2 * cos + x1 * sin], axis=-1)

def causal_attention(q, k, v):
    b, h, s, d = q.shape
    nb = s // Q_BLOCK
    scale = d ** -0.5
    qb = q.reshape(b, h, nb, Q_BLOCK, d).transpose(2, 0, 1, 3, 4)
    kpos = jnp.arange(s)

    def one_block(args):
        qi, i = args
        sc = jnp.einsum('bhqd,bhkd->bhqk', qi, k).astype(jnp.float32) * scale
        qpos = i * Q_BLOCK + jnp.arange(Q_BLOCK)
        mask = kpos[None, :] <= qpos[:, None]
        sc = jnp.where(mask, sc, jnp.finfo(jnp.float32).min)
        p = jax.nn.softmax(sc, axis=-1)
        return jnp.einsum('bhqk,bhkd->bhqd', p.astype(v.dtype), v)

    out = lax.map(one_block, (qb, jnp.arange(nb)))
    return out.transpose(1, 0, 3, 2, 4).reshape(b, s, h * v.shape[-1])

def ssd_chunked(x, dt, a, bm, cm):
    b, l, h, p = x.shape
    rep = h // bm.shape[2]
    nc = l // CHUNK_2
    xf = x.astype(jnp.float32)
    xdt = xf * dt[..., None]
    adt = dt * a
    bh = jnp.repeat(bm.astype(jnp.float32), rep, axis=2)
    ch = jnp.repeat(cm.astype(jnp.float32), rep, axis=2)
    n = bh.shape[-1]
    xc = xdt.reshape(b, nc, CHUNK_2, h, p)
    bc = bh.reshape(b, nc, CHUNK_2, h, n)
    cc = ch.reshape(b, nc, CHUNK_2, h, n)
    acs = jnp.cumsum(adt.reshape(b, nc, CHUNK_2, h), axis=2)
    seg = acs[:, :, :, None, :] - acs[:, :, None, :, :]
    tri = jnp.tril(jnp.ones((CHUNK_2, CHUNK_2), dtype=bool))[None, None, :, :, None]
    lmat = jnp.exp(jnp.where(tri, seg, -jnp.inf))
    scores = jnp.einsum('bclhn,bcshn->bclsh', cc, bc) * lmat
    y_diag = jnp.einsum('bclsh,bcshp->bclhp', scores, xc)
    decay_states = jnp.exp(acs[:, :, -1:, :] - acs)
    states = jnp.einsum('bcshn,bcsh,bcshp->bchpn', bc, decay_states, xc)
    chunk_decay = jnp.exp(acs[:, :, -1, :])

    def step(carry, inp):
        s_c, d_c = inp
        new = d_c[:, :, None, None] * carry + s_c
        return new, carry

    init = jnp.zeros((b, h, p, n), jnp.float32)
    _, prev = lax.scan(step, init, (states.transpose(1, 0, 2, 3, 4), chunk_decay.transpose(1, 0, 2)))
    prev = prev.transpose(1, 0, 2, 3, 4)
    y_off = jnp.einsum('bclhn,bchpn,bclh->bclhp', cc, prev, jnp.exp(acs))
    return (y_diag + y_off).reshape(b, l, h, p)

def hybrid_mixer(h, cos, sin, w_in, q_a_norm_w, w_q_up, kv_a_norm_w, w_kv_up,
                 q_nope_norm_w, q_pe_norm_w, k_nope_norm_w, k_pe_norm_w,
                 conv_w, conv_b, dt_bias, a_log, d_skip, ssd_norm_w, w_out):
    b, s, _ = h.shape
    proj = h @ w_in
    cuts = np.cumsum([Q_LORA_RANK, KV_LORA_RANK, QK_ROPE_DIM, D_SSD, D_CONV])
    q_a, kv_a, k_pe, z, xbc, dt_raw = jnp.split(proj, [int(i) for i in cuts], axis=-1)

    q = (rmsnorm_2(q_a, q_a_norm_w) @ w_q_up).reshape(b, s, MLA_HEADS, QK_HEAD_DIM)
    q_nope, q_pe = jnp.split(q, [QK_NOPE_DIM], axis=-1)
    kv = (rmsnorm_2(kv_a, kv_a_norm_w) @ w_kv_up).reshape(b, s, MLA_HEADS, QK_NOPE_DIM + V_HEAD_DIM)
    k_nope, v = jnp.split(kv, [QK_NOPE_DIM], axis=-1)
    q_nope = rmsnorm_2(q_nope, q_nope_norm_w)
    q_pe = rope(rmsnorm_2(q_pe, q_pe_norm_w), cos, sin)
    k_nope = rmsnorm_2(k_nope, k_nope_norm_w)
    k_pe = rope(rmsnorm_2(k_pe[:, :, None, :], k_pe_norm_w), cos, sin)
    q_full = jnp.concatenate([q_nope, q_pe], axis=-1)
    k_full = jnp.concatenate([k_nope, jnp.broadcast_to(k_pe, (b, s, MLA_HEADS, QK_ROPE_DIM))], axis=-1)
    attn_out = causal_attention(q_full.transpose(0, 2, 1, 3), k_full.transpose(0, 2, 1, 3),
                                v.transpose(0, 2, 1, 3))

    xbc = lax.conv_general_dilated(xbc, conv_w[:, None, :], window_strides=(1,),
                                   padding=[(CONV_WIDTH - 1, 0)],
                                   dimension_numbers=('NWC', 'WIO', 'NWC'),
                                   feature_group_count=D_CONV)
    xbc = jax.nn.silu(xbc + conv_b)
    xs, bm, cm = jnp.split(xbc, [D_SSD, D_SSD + SSD_GROUPS * SSD_STATE], axis=-1)
    xs = xs.reshape(b, s, SSD_HEADS, SSD_HEAD_DIM)
    bm = bm.reshape(b, s, SSD_GROUPS, SSD_STATE)
    cm = cm.reshape(b, s, SSD_GROUPS, SSD_STATE)
    dt = jax.nn.softplus(dt_raw.astype(jnp.float32) + dt_bias.astype(jnp.float32))
    a = -jnp.exp(a_log.astype(jnp.float32))
    y = ssd_chunked(xs, dt, a, bm, cm) + d_skip.astype(jnp.float32)[:, None] * xs.astype(jnp.float32)
    y = y.astype(h.dtype).reshape(b, s, D_SSD)
    yg = (y * jax.nn.silu(z)).reshape(b, s, SSD_GROUPS, D_SSD // SSD_GROUPS)
    yg = rmsnorm_2(yg, jnp.ones((D_SSD // SSD_GROUPS,), h.dtype)).reshape(b, s, D_SSD) * ssd_norm_w

    return jnp.concatenate([attn_out, yg], axis=-1) @ w_out

def swiglu_2(h, w_gate_up, w_down):
    g, u = jnp.split(h @ w_gate_up, 2, axis=-1)
    return (jax.nn.silu(g) * u) @ w_down

def second_inputs(seed: int = 0) -> dict:
    key = jax.random.key(seed)
    ks = jax.random.split(key, 32)
    f32 = jnp.float32

    def nrm(k, shape, scale):
        return jax.random.normal(k, shape, f32) * scale

    def gain(k, shape):
        return 1.0 + 0.05 * jax.random.normal(k, shape, f32)

    L = DEPTH
    dt0 = jnp.exp(jax.random.uniform(ks[18], (L, SSD_HEADS), f32, np.log(1e-3), np.log(1e-1)))
    dt_bias = dt0 + jnp.log(-jnp.expm1(-dt0))
    pos_off = jax.random.randint(ks[2], (BATCH, 1), 0, 1024, dtype=jnp.int32)
    return {
        "x": nrm(ks[0], (BATCH, SEQ, D_MODEL), 1.0),
        "c": nrm(ks[1], (BATCH, D_MODEL), 1.0),
        "positions": pos_off + jnp.arange(SEQ, dtype=jnp.int32)[None, :],
        "norm1_w": gain(ks[3], (L, D_MODEL)),
        "norm2_w": gain(ks[4], (L, D_MODEL)),
        "w_ada": nrm(ks[5], (L, D_MODEL, N_MOD * D_MODEL), 0.5 * D_MODEL ** -0.5),
        "b_ada": nrm(ks[6], (L, N_MOD * D_MODEL), 0.01),
        "w_in": nrm(ks[7], (L, D_MODEL, D_IN), D_MODEL ** -0.5),
        "q_a_norm_w": gain(ks[8], (L, Q_LORA_RANK)),
        "w_q_up": nrm(ks[9], (L, Q_LORA_RANK, MLA_HEADS * QK_HEAD_DIM), Q_LORA_RANK ** -0.5),
        "kv_a_norm_w": gain(ks[10], (L, KV_LORA_RANK)),
        "w_kv_up": nrm(ks[11], (L, KV_LORA_RANK, MLA_HEADS * (QK_NOPE_DIM + V_HEAD_DIM)), KV_LORA_RANK ** -0.5),
        "q_nope_norm_w": gain(ks[12], (L, QK_NOPE_DIM)),
        "q_pe_norm_w": gain(ks[13], (L, QK_ROPE_DIM)),
        "k_nope_norm_w": gain(ks[14], (L, QK_NOPE_DIM)),
        "k_pe_norm_w": gain(ks[15], (L, QK_ROPE_DIM)),
        "conv_w": nrm(ks[16], (L, CONV_WIDTH, D_CONV), CONV_WIDTH ** -0.5),
        "conv_b": nrm(ks[17], (L, D_CONV), 0.01),
        "dt_bias": dt_bias,
        "a_log": jnp.log(jax.random.uniform(ks[19], (L, SSD_HEADS), f32, 1.0, 16.0)),
        "d_skip": 1.0 + 0.1 * jax.random.normal(ks[20], (L, SSD_HEADS), f32),
        "ssd_norm_w": gain(ks[21], (L, D_SSD)),
        "w_out": nrm(ks[22], (L, D_MIX, D_MODEL), D_MIX ** -0.5),
        "w_gate_up": nrm(ks[23], (L, D_MODEL, 2 * D_FF_2), D_MODEL ** -0.5),
        "w_down": nrm(ks[24], (L, D_FF_2, D_MODEL), D_FF_2 ** -0.5),
    }

def second_block(x, c, positions, norm1_w, norm2_w, w_ada, b_ada, w_in, q_a_norm_w, w_q_up,
              kv_a_norm_w, w_kv_up, q_nope_norm_w, q_pe_norm_w, k_nope_norm_w, k_pe_norm_w,
              conv_w, conv_b, dt_bias, a_log, d_skip, ssd_norm_w, w_out, w_gate_up, w_down):
    inv_freq = 1.0 / (ROPE_THETA ** (jnp.arange(0, QK_ROPE_DIM, 2, dtype=jnp.float32) / QK_ROPE_DIM))
    ang = positions.astype(jnp.float32)[..., None] * inv_freq
    cos = jnp.cos(ang)[:, :, None, :].astype(x.dtype)
    sin = jnp.sin(ang)[:, :, None, :].astype(x.dtype)
    c_act = jax.nn.silu(c)
    for l in range(DEPTH):
        mod = (c_act @ w_ada[l] + b_ada[l])[:, None, :]
        sh1, sc1, g1, sh2, sc2, g2 = jnp.split(mod, N_MOD, axis=-1)
        h = rmsnorm_2(x, norm1_w[l]) * (1.0 + sc1) + sh1
        x = x + g1 * hybrid_mixer(h, cos, sin, w_in[l], q_a_norm_w[l], w_q_up[l], kv_a_norm_w[l],
                                  w_kv_up[l], q_nope_norm_w[l], q_pe_norm_w[l], k_nope_norm_w[l],
                                  k_pe_norm_w[l], conv_w[l], conv_b[l], dt_bias[l], a_log[l],
                                  d_skip[l], ssd_norm_w[l], w_out[l])
        h = rmsnorm_2(x, norm2_w[l]) * (1.0 + sc2) + sh2
        x = x + g2 * swiglu_2(h, w_gate_up[l], w_down[l])
    return x


def setup_inputs(seed=0):
    out = dict(first_inputs(seed))
    for name, value in second_inputs(seed + 1).items():
        if name != "x":
            out[name + "_2"] = value
    return out


def reference(
    x, p, ffn_norm, ffn_w1, ffn_w3, ffn_w2, mix_norm, ple_norm, ple_proj, ple_gate, final_norm,
    m0_w_in, gla_gate_up, gla_gate_bias, gla_head_norm, lru_conv_w, lru_conv_b, lru_wa, lru_ba,
    lru_wx, lru_bx, lru_lambda, m0_w_out, m1_w_in, hgrn_lb_logits, hgrn_head_norm, m1_w_out,
    c_2, positions_2, norm1_w_2, norm2_w_2, w_ada_2, b_ada_2, w_in_2, q_a_norm_w_2, w_q_up_2,
    kv_a_norm_w_2, w_kv_up_2, q_nope_norm_w_2, q_pe_norm_w_2, k_nope_norm_w_2, k_pe_norm_w_2,
    conv_w_2, conv_b_2, dt_bias_2, a_log_2, d_skip_2, ssd_norm_w_2, w_out_2, w_gate_up_2,
    w_down_2,
):
    x = first_block(
        x, p, ffn_norm, ffn_w1, ffn_w3, ffn_w2, mix_norm, ple_norm, ple_proj, ple_gate,
        final_norm, m0_w_in, gla_gate_up, gla_gate_bias, gla_head_norm, lru_conv_w, lru_conv_b,
        lru_wa, lru_ba, lru_wx, lru_bx, lru_lambda, m0_w_out, m1_w_in, hgrn_lb_logits,
        hgrn_head_norm, m1_w_out,
    )
    return second_block(
        x, c_2, positions_2, norm1_w_2, norm2_w_2, w_ada_2, b_ada_2, w_in_2, q_a_norm_w_2,
        w_q_up_2, kv_a_norm_w_2, w_kv_up_2, q_nope_norm_w_2, q_pe_norm_w_2, k_nope_norm_w_2,
        k_pe_norm_w_2, conv_w_2, conv_b_2, dt_bias_2, a_log_2, d_skip_2, ssd_norm_w_2, w_out_2,
        w_gate_up_2, w_down_2,
    )


_drawn_inputs = setup_inputs


def setup_inputs(seed=0):
    import zlib

    import numpy as np

    out = dict(_drawn_inputs(seed))
    spreads = {}
    factors = {'ple_norm': 4.833,
     'gla_gate_bias': 3.187,
     'gla_head_norm': 2.734,
     'lru_conv_b': 2.976,
     'lru_ba': 8.0,
     'lru_bx': 8.0,
     'hgrn_lb_logits': 8.0,
     'hgrn_head_norm': 2.746,
     'norm2_w_2': 2.731,
     'b_ada_2': 3.376,
     'q_a_norm_w_2': 8.0,
     'kv_a_norm_w_2': 8.0,
     'q_nope_norm_w_2': 8.0,
     'q_pe_norm_w_2': 8.0,
     'k_nope_norm_w_2': 8.0,
     'k_pe_norm_w_2': 8.0,
     'conv_b_2': 8.0,
     'd_skip_2': 3.068,
     'ssd_norm_w_2': 4.032}
    for name, (base, spread) in spreads.items():
        noise = np.random.default_rng([zlib.crc32(name.encode()), seed]).standard_normal(out[name].shape)
        drawn = base * np.exp(spread * noise) if base else spread * noise
        out[name] = __import__('jax').numpy.asarray(drawn.astype(out[name].dtype))
    for name, factor in factors.items():
        out[name] = (out[name] * factor).astype(out[name].dtype)
    return out
```

```python
import numpy as np
from contextlib import ExitStack

import concourse.bass as bass
from concourse import mybir

F32 = mybir.dt.float32
F32R = mybir.dt.float32r
I32 = mybir.dt.int32
ALU = mybir.AluOpType
ACT = mybir.ActivationFunctionType
AX = mybir.AxisListType
MUL, ADD, SUB, MAX, MIN = ALU.mult, ALU.add, ALU.subtract, ALU.max, ALU.min

D, S, NF, FT, EPS = 1024, 512, 2816, 22, 1e-6
RAW, SUBS = 3, 3


class Queue:

    def __init__(self, sem):
        self.sem, self.n, self.ops, self.seen = sem, 0, [], {}

    def wait(self, *events):
        for e in events:
            if e is None:
                continue
            if isinstance(e, list):
                self.wait(*e)
                continue
            sem, v = e
            if self.seen.get(sem.name, 0) < v:
                self.seen[sem.name] = v
                self.ops.append((None, sem, v))

    def do(self, fn, *events):
        self.wait(*events)
        self.n += 1
        self.ops.append((fn, self.sem, 1))
        return self.sem, self.n

    def dma(self, fn, sem, *events):
        self.wait(*events)
        self.ops.append((fn, sem, 16))

    def quiet(self, fn):
        self.ops.append((fn, None, 0))

    def run(self, eng):
        for fn, sem, v in self.ops:
            if fn is None:
                eng.wait_ge(sem, v)
            elif sem is None:
                fn(eng)
            else:
                fn(eng).then_inc(sem, v)


class Act(Queue):
    def f(self, out, in_, func, *ev, **kw):
        return self.do(lambda e: e.activation(out, in_, func, **kw), *ev)


class Alu(Queue):
    def tt(self, out, a, b, op, *ev):
        return self.do(lambda e: e.tensor_tensor(out, a, b, op), *ev)

    def ts(self, out, a, s1, op0, *ev, s2=None, op1=None):
        if op1 is None:
            return self.do(lambda e: e.tensor_scalar(out, a, s1, None, op0), *ev)
        return self.do(lambda e: e.tensor_scalar(out, a, s1, s2, op0, op1), *ev)

    def stt(self, out, a, s, b, op0, op1, *ev):
        return self.do(lambda e: e.scalar_tensor_tensor(out=out, in0=a, scalar=s, in1=b, op0=op0, op1=op1), *ev)

    def copy(self, out, a, *ev):
        return self.do(lambda e: e.tensor_copy(out, a), *ev)

    def recip(self, out, a, *ev):
        return self.do(lambda e: e.reciprocal(out, a), *ev)

    def scan(self, out, m, a, *ev):
        return self.do(lambda e: e.tensor_tensor_scan(out, m, a, 0.0, MUL, ADD), *ev)

    def rmax(self, out, a, *ev):
        return self.do(lambda e: e.tensor_reduce(out, a, AX.X, MAX), *ev)

    def set(self, out, v, *ev):
        return self.do(lambda e: e.memset(out, v), *ev)

    def select(self, out, pattern, base, mult, op, fill, *ev):
        return self.do(lambda e: e.affine_select(out=out, in_=out, compare_op=op, fill=fill, base=base,
                                                 pattern=pattern, channel_multiplier=mult), *ev)


class Pe(Queue):
    def mms(self, items, *ev):
        self.wait(*ev)
        for it in items[:-1]:
            self.quiet(self.one(it))
        return self.do(self.one(items[-1]))

    @staticmethod
    def one(it):
        out, l, r, a, z = it
        return lambda e: e.matmul(out, l, r, start=a, stop=z, skip_group_check=True)

    def trs(self, items, *ev):
        self.wait(*ev)
        for o, i, d in items[:-1]:
            self.quiet(lambda e, o=o, i=i, d=d: e.transpose(o, i, d))
        o, i, d = items[-1]
        return self.do(lambda e: e.transpose(o, i, d))


class Bank:
    def __init__(self, ap):
        self.ap, self.free, self.busy = ap, [], False

    def rel(self, *ev):
        self.free, self.busy = list(ev), False


class Sub:
    pass


INS = ['x', 'p', 'ffn_norm', 'ffn_w1', 'ffn_w3', 'ffn_w2', 'mix_norm', 'ple_norm', 'ple_proj', 'ple_gate',
       'final_norm', 'm0_w_in', 'gla_gate_up', 'gla_gate_bias', 'gla_head_norm', 'lru_conv_w', 'lru_conv_b',
       'lru_wa', 'lru_ba', 'lru_wx', 'lru_bx', 'lru_lambda', 'm0_w_out', 'm1_w_in', 'hgrn_lb_logits',
       'hgrn_head_norm', 'm1_w_out', 'c_2', 'positions_2', 'norm1_w_2', 'norm2_w_2', 'w_ada_2', 'b_ada_2',
       'w_in_2', 'q_a_norm_w_2', 'w_q_up_2', 'kv_a_norm_w_2', 'w_kv_up_2', 'q_nope_norm_w_2',
       'q_pe_norm_w_2', 'k_nope_norm_w_2', 'k_pe_norm_w_2', 'conv_w_2', 'conv_b_2', 'dt_bias_2', 'a_log_2',
       'd_skip_2', 'ssd_norm_w_2', 'w_out_2', 'w_gate_up_2', 'w_down_2', 'inv_freq']

STAGES = [("ffn", 0, 0), ("mix0",), ("ffn", 0, 1), ("ple", 0), ("ffn", 1, 0), ("mix1",), ("ffn", 1, 1),
          ("ple", 1), ("final",), ("mix2", 0), ("ffn2", 0), ("mix2", 1), ("ffn2", 1)]
ADA_PER_FFN = 12


def build(nc, I, out, stages):
    ctx = ExitStack()
    with ctx:
        def sem(name):
            return ctx.enter_context(nc.semaphore(name))

        off = [nc.sbuf_base + (-nc.sbuf_base) % 64]

        def sb(name, shape, dt=F32, alias=None):
            n = 4 * int(np.prod(shape[1:]))
            o = off[0] if alias is None else alias
            if alias is None:
                off[0] += n + (-n) % 32
            t = place(name, shape, dt, o)
            return t, o

        def place(name, shape, dt, o):
            return nc.alloc_sbuf_tensor_at(name, shape, dt, offset=o)

        x, _ = sb("x", [128, 8, S])
        hh, o_h = sb("hh", [128, 8, S], F32R)
        hl, o_l = sb("hl", [128, 8, S], F32R)
        sp, _ = sb("sp", [128, 16, S], F32, o_h)
        ar, o_a = sb("ar", [128, 2 * FT, S])
        uh, _ = sb("uh", [128, FT, S], F32R, o_a)
        ul, _ = sb("ul", [128, FT, S], F32R, o_a + FT * S * 4)
        ch, _ = sb("ch", [128, 8, S], F32R, o_a)
        cl, _ = sb("cl", [128, 8, S], F32R, o_a + 8 * S * 4)
        raw = [sb(f"raw{i}", [128, 2048])[0] for i in range(RAW)]
        wh = [sb(f"wh{i}", [128, 1024], F32R)[0] for i in range(SUBS)]
        wl = [sb(f"wl{i}", [128, 1024], F32R)[0] for i in range(SUBS)]
        VT, _ = sb("VT", [128, 3 * 128])
        ident, _ = sb("ident", [128, 128])
        ones, _ = sb("ones", [128, 128])
        tri, _ = sb("tri", [128, 128])
        neg, _ = sb("neg", [128, 128])
        perm, _ = sb("perm", [128, 128])
        Z = {n: sb(f"Z{n}", [128, 64])[0] for n in ("256", "128", "64", "32", "k")}
        R, _ = sb("R", [128, S])
        sq = [sb(f"sq{i}", [128, S])[0] for i in range(2)]
        acc, _ = sb("acc", [128, S])
        T1 = [sb(f"T1{i}", [128, S])[0] for i in range(2)]
        T3 = [sb(f"T3{i}", [128, S])[0] for i in range(2)]
        ada = [sb("ada", [128, 256])[0]]
        mod, _ = sb("mod", [128, 96])
        G, _ = sb("G", [128, 8])
        small, _ = sb("small", [128, 160])
        assert off[0] <= nc.sbuf_top, (off[0], nc.sbuf_top)

        psum = [ctx.enter_context(nc.psum_tensor(f"ps{i}", [128, S], F32)) for i in range(8)]

        act, dve, pool, pe, sp_q = (C(sem(n)) for C, n in
                                    ((Act, "s_act"), (Alu, "s_dve"), (Alu, "s_pool"), (Pe, "s_pe"), (Queue, "s_sp")))
        s_raw = [sem(f"s_raw{i}") for i in range(RAW)]
        s_vec, s_x, s_misc, s_out = sem("s_vec"), sem("s_x"), sem("s_misc"), sem("s_out")
        misc = [0]

        def A(i, n=1):
            return ar[:, i, :] if n == 1 else ar[:, i:i + n, :]

        def misc_dma(dst, src, *ev):
            act.dma(lambda e: e.dma_start(dst, src), s_misc, *ev)
            misc[0] += 16
            return s_misc, misc[0]

        banks = [Bank(p) for p in psum]
        turn = [0]

        def bank():
            for _ in range(8):
                b = banks[turn[0] % 8]
                turn[0] += 1
                if not b.busy:
                    b.busy = True
                    return b
            raise AssertionError("no bank")

        chunks, subs = [], []

        def chunk(key, kt, width, pieces, parts, kind="mm"):
            n = len(chunks)
            chunks.append((kt, width, pieces, len(parts)))
            for i, pt in enumerate(parts):
                subs.append((key, n, *pt, *((0, kt) if len(pt) == 2 else ()), kind, i == len(parts) - 1))

        def wide(key, W, c0, n, k0=0, kt=8):
            for c in range(0, n, 256):
                w = min(256, n - c)
                chunk(key, kt, w, [(0, W[k0:k0 + kt * 128, c0 + c:c0 + c + w])],
                      [(i, 128) for i in range(0, w, 128)])

        def tall(key, W, c0, n):
            for c in range(c0, c0 + n, 512):
                for k in range(2):
                    chunk(key, 4, 512, [(0, W[512 * k:512 * k + 512, c:c + 512])], [(0, 512, 0, 2), (0, 512, 2, 2)])

        ada_next = [0]

        def plan_ada(n):
            for _ in range(n):
                i = ada_next[0]
                if i < 48:
                    l, c = divmod(i, 24)
                    chunk(("ada", i), 8, 256, [(0, I['w_ada_2'][l][:, c * 256:c * 256 + 256])], [(0, 256)], "ada")
                    ada_next[0] += 1

        def plan_ffn(key, w1, w3, w2, with_ada):
            for j in range(11):
                wide(key, w1, j * 256, 256)
                wide(key, w3, j * 256, 256)
                if with_ada:
                    plan_ada(1)
            if with_ada:
                plan_ada(ADA_PER_FFN - 11)
            for m in range(4):
                for k0, kt in ((0, 8), (8, 8), (16, 6)):
                    wide(key, w2, m * 256, 256, k0 * 128, kt)

        for st in stages:
            if st[0] == "ffn":
                plan_ffn(st, I['ffn_w1'][st[1], st[2]], I['ffn_w3'][st[1], st[2]], I['ffn_w2'][st[1], st[2]], True)
            elif st[0] == "mix0":
                W = I['m0_w_in'][0]
                for c, n in ((1536, 128), (256, 256), (0, 256)):
                    wide(st, W, c, n)
                tall(st, W, 512, 512)
                for c in (1552, 1024, 2064):
                    wide(st, W, c, 512)
                wide(st, I['m0_w_out'][0], 0, 1024)
            elif st[0] == "mix1":
                W = I['m1_w_in'][0]
                wide(st, W, 1024, 1024)
                tall(st, W, 2048, 1024)
                wide(st, W, 0, 1024)
                wide(st, W, 3072, 1024)
                wide(st, I['m1_w_out'][0], 0, 1024)
            elif st[0] == "ple":
                wide(st, I['ple_gate'][st[1]], 0, 1024)
                chunk(st, 2, 1024, [(0, I['ple_proj'][st[1]])], [(0, 512), (512, 512)])
            elif st[0] == "mix2":
                l = st[1]
                W = I['w_in_2'][l]
                plan_ada(48 - ada_next[0])
                chunk(st, 8, 128, [(0, W[:, 384:416]), (32, W[:, 1952:1960]), (40, W[:, 416:504])], [(0, 128)])
                wide(st, W, 0, 256)
                wide(st, W, 256, 128)
                wide(st, W, 928, 1024)
                Wq = I['w_q_up_2'][l].rearrange("k (h n) -> k h n", n=96)
                chunk(st, 2, 768, [(384 * s + c, Wq[:, 4 * s:4 * s + 4, a:z]) for s in range(2)
                                   for c, a, z in ((0, 0, 64), (256, 64, 96))], [(0, 384), (384, 384)])
                Wk = I['w_kv_up_2'][l].rearrange("k (h n) -> k h n", n=128)
                chunk(st, 1, 1024, [(0, Wk[:, :, 0:64]), (512, Wk[:, :, 64:128])], [(0, 1024)])
                wide(st, W, 416, 512)
                wide(st, I['w_out_2'][l], 0, 1024)
            elif st[0] == "ffn2":
                l = st[1]
                W = I['w_gate_up_2'][l]
                plan_ffn(st, W[:, 0:NF], W[:, NF:2 * NF], I['w_down_2'][l], False)
        if any(st[0] == "mix2" for st in stages):
            assert ada_next[0] == 48

        raw_free = [[] for _ in range(RAW)]
        raw_n = [0] * RAW
        raw_ev = {}
        sent = [0]

        def send():
            n = sent[0]
            if n >= len(chunks):
                return
            sent[0] += 1
            kt, width, pieces, _ = chunks[n]
            s = n % RAW
            v = raw[s][:, 0:kt * width].rearrange("p (t n) -> p t n", t=kt)
            sp_q.wait(raw_free[s])
            for c, src in pieces:
                if len(src.shape) == 2:
                    moves = [(v[:, :, c:c + src.shape[1]], src.rearrange("(t p) n -> p t n", p=128))]
                else:
                    w, n_h = src.shape[1] * src.shape[2], src.shape[2]
                    moves = [(v[:, t, c:c + w].rearrange("p (h n) -> p h n", n=n_h), src[128 * t:128 * t + 128])
                             for t in range(kt)]
                for d, r in moves:
                    sp_q.dma(lambda e, d=d, r=r: e.dma_start(d, r), s_raw[s])
                    raw_n[s] += 16
            raw_ev[n] = (s_raw[s], raw_n[s])

        sub_free = [[] for _ in range(SUBS)]
        ready = {}
        done_subs = [0, 0]
        ada_free = [[]]
        ada_wait = []
        mod_ev = [None]

        def split(limit):
            while done_subs[0] < len(subs):
                key, n, c, w, t0, tn, kind, last = subs[done_subs[0]]
                if kind == "mm" and done_subs[1] > limit:
                    return
                if kind == "ada" and consts_ready[0] is None:
                    return
                done_subs[0] += 1
                kt, width, _, _ = chunks[n]
                src = raw[n % RAW][:, 0:kt * width].rearrange("p (t n) -> p t n", t=kt)[:, t0:t0 + tn, c:c + w]
                if kind == "mm":
                    g = done_subs[1]
                    done_subs[1] += 1
                    s = g % SUBS
                    hi = wh[s][:, 0:tn * w].rearrange("p (t n) -> p t n", t=tn)
                    lo = wl[s][:, 0:tn * w].rearrange("p (t n) -> p t n", t=tn)
                    e1 = act.f(hi, src, ACT.Copy, raw_ev[n], sub_free[s])
                    e2 = dve.tt(lo, src, hi.bitcast(F32), SUB, e1)
                    t = Sub()
                    t.key, t.hi, t.lo, t.ev, t.slot, t.kt = key, hi, lo, [e1, e2], s, tn
                    ready[g] = t
                    e = [e1, e2]
                else:
                    ada_sums()
                    i = key[1]
                    a = ada[0]
                    e = dve.ts(a[:, :], src[:, 0, :], c_act[:, 0:1], MUL, raw_ev[n], ada_free[0], consts_ready[0])
                    for t in range(1, 8):
                        e = dve.stt(a[:, :], src[:, t, :], c_act[:, t:t + 1], a[:, :], MUL, ADD, e)
                    ada_wait.append((i, a, e, used[0]))
                    e = [e]
                if last:
                    raw_free[n % RAW] = e
                    send()

        def ada_sums(late=0):
            while ada_wait and ada_wait[0][3] + late <= used[0]:
                i, a, e, _ = ada_wait.pop(0)
                b = bank()
                e = pe.mms([(b.ap[:, h:h + 1], a[:, 128 * h:128 * h + 128], ones[:, 0:1], True, True)
                            for h in range(2)], e, b.free)
                ada_free[0] = [e]
                mod_ev[0] = dve.tt(mod[:, 2 * i:2 * i + 2], b.ap[:, 0:2], VT[:, vec_at["b_ada"] + 2 * i:vec_at["b_ada"] + 2 * i + 2], ADD, e)
                b.rel(mod_ev[0])

        used = [0]

        def take(key):
            g = used[0]
            used[0] += 1
            ada_sums(2)
            split(g + SUBS - 1)
            t = ready.pop(g)
            assert t.key == key, (t.key, key)
            return t

        def give(t, e):
            sub_free[t.slot] = [e]

        def three(out, w, k, cols, a_h, a_l, start, stop, tok=False):
            H, L = w.hi[:, k, cols], w.lo[:, k, cols]
            if tok:
                return [(out, a_h, L, start, False), (out, a_l, H, False, False), (out, a_h, H, False, stop)]
            return [(out, L, a_h, start, False), (out, H, a_l, False, False), (out, H, a_h, False, stop)]

        C128 = slice(0, 128)

        def product(key, ah, al, ev_k):
            w, b = take(key), bank()
            pe.wait(w.ev, b.free)
            for k in range(w.kt):
                e = pe.mms(three(b.ap[:, :], w, k, C128, ah[:, k, :], al[:, k, :], k == 0, k == w.kt - 1), ev_k[k])
            give(w, e)
            return b, e

        def product_tok(key, ah, al, ev_k):
            bs = [bank() for _ in range(4)]
            es = [None] * 4
            for q in range(4):
                w = take(key)
                pe.wait(w.ev, ev_k)
                for t, b in enumerate(bs):
                    pe.wait(b.free)
                    r = slice(128 * t, 128 * t + 128)
                    its = []
                    for j in range(2):
                        k = 2 * q + j
                        its += three(b.ap[:, :], w, j, slice(0, 512), ah[:, k, r], al[:, k, r], k == 0, k == 7, True)
                    es[t] = pe.mms(its)
                give(w, es[3])
            return list(zip(bs, es))

        z0 = pool.set(ident[:, :], 0.0)
        e_id = pool.select(ident[:, :], [[-1, 128]], 0, 1, ALU.not_equal, 1.0, z0)
        e_on = pool.set(ones[:, :], 1.0)
        t0 = pool.set(tri[:, :], 1.0)
        e_tri = pool.select(tri[:, :], [[1, 128]], 0, -1, ALU.is_ge, 0.0, t0)
        t0 = pool.set(neg[:, :], 0.0)
        e_neg = pool.select(neg[:, :], [[-1, 128]], 0, 1, ALU.is_ge, -1e30, t0)
        t0 = pool.set(perm[:, :], 0.0)
        pv = perm[:, :].rearrange("p (a b c) -> p a b c", a=4, b=2)
        t0 = pool.select(pv[:, :, 0, :], [[-32, 4], [-1, 16]], -16, 1, ALU.not_equal, -1.0, t0)
        e_perm = pool.select(pv[:, :, 1, :], [[-32, 4], [-1, 16]], 0, 1, ALU.not_equal, 1.0, t0)
        for n in Z:
            e = pool.set(Z[n][:, :], 0.0)
        e = pool.set(Z["256"][:, 32:33], 1 / 256, e)
        e = pool.set(Z["128"][:, 32:33], 1 / 128, e)
        e = pool.set(Z["k"][:, 32:33], 1 / 32, e)
        for h in range(2):
            e = pool.set(Z["64"][64 * h:64 * h + 64, 32 + h:33 + h], 1 / 64, e)
        for h in range(4):
            e_Z = e = pool.set(Z["32"][32 * h:32 * h + 32, 32 + h:33 + h], 1 / 32, e)
        c_act = small[:, 0:8]
        clam = small[:, 8:12]
        lnlb, ln1lb, onelb, dif = (small[:, 12 + 8 * i:20 + 8 * i] for i in range(4))
        acol = small[:, 44:46]
        dskip = small[:, 46:54]
        invf = small[:, 54:55]
        mhalf = small[:, 55:59]
        tk = small[:, 60:64]
        rtok = small[:, 64:68]
        t8 = [small[:, 72 + 8 * i:80 + 8 * i] for i in range(6)]
        sm = small[:, 120:160]
        e_mh = pool.set(mhalf, -0.5, e_Z)

        vec_at, rows, zr = {}, [0, 128, 256], []
        V = ar[:, 40, 0:384].rearrange("p (v n) -> p v n", v=3)
        e_v0 = pool.set(ar[:, 40, 0:384], 0.0, e_mh)
        n_vec = [0]

        def vec(name, tile, src=None, n=None, pieces=None):
            r = rows[tile]
            p = r - 128 * tile
            vec_at[name] = r
            for dst, s in pieces or [((p, p + n, 0, 128), src)]:
                if pieces:
                    dst = (p + dst[0], p + dst[1], dst[2], dst[3])
                act.dma(lambda e, d=V[dst[0]:dst[1], tile, dst[2]:dst[3]], s=s: e.dma_start(d, s), s_vec, e_v0)
                n_vec[0] += 16
            rows[tile] += n
            assert rows[tile] <= 128 * (tile + 1)

        def r128(ap, pat, **kw):
            return ap.rearrange(pat, **kw)

        xs_in = ar[:, 0:8, :].rearrange("p (b h) n -> p b (h n)", b=4)
        xin = I['x'][0].rearrange("(b p) d -> p b d", p=128)
        n_x = [0]
        for b in range(4):
            sp_q.dma(lambda e, b=b: e.dma_start(xs_in[:, b, :], xin[:, b, :]), s_x)
        for _ in range(RAW):
            send()
        vec("ffn_norm", 0, r128(I['ffn_norm'], "l s (t p) -> (l s t) p", p=128), 32)
        vec("mix_norm", 0, r128(I['mix_norm'], "l (t p) -> (l t) p", p=128), 16)
        vec("ple_norm", 0, r128(I['ple_norm'], "l (t p) -> (l t) p", p=128), 16)
        vec("final_norm", 0, r128(I['final_norm'], "(t p) -> t p", p=128), 8)
        vec("gla_gate_bias", 0, r128(I['gla_gate_bias'], "o (t p) -> (o t) p", p=128), 2)
        vec("gla_head_norm", 0, I['gla_head_norm'], 1)
        vec("lru_conv_w", 0, r128(I['lru_conv_w'], "o w (t p) -> (o w t) p", p=128), 16)
        for n in ("lru_conv_b", "lru_ba", "lru_bx", "lru_lambda"):
            vec(n, 0, r128(I[n], "o (t p) -> (o t) p", p=128), 4)
        vec("hgrn_lb_logits", 0, r128(I['hgrn_lb_logits'], "l (t p) -> (l t) p", p=128), 16)
        vec("hgrn_head_norm", 0, I['hgrn_head_norm'], 1)
        vec("norm1", 1, r128(I['norm1_w_2'], "l (t p) -> (l t) p", p=128), 16)
        vec("norm2", 1, r128(I['norm2_w_2'], "l (t p) -> (l t) p", p=128), 16)
        vec("b_ada", 1, r128(I['b_ada_2'], "l (t p) -> (l t) p", p=128), 96)
        vec("q_a", 2, r128(I['q_a_norm_w_2'], "l (t p) -> (l t) p", p=128), 4)
        vec("kv_a", 2, I['kv_a_norm_w_2'], 2)
        vec("conv_w", 2, r128(I['conv_w_2'], "l w (t p) -> (l w t) p", p=128), 64)
        vec("conv_b", 2, r128(I['conv_b_2'], "l (t p) -> (l t) p", p=128), 16)
        vec("ssd_norm", 2, r128(I['ssd_norm_w_2'], "l (t p) -> (l t) p", p=128), 8)
        vec("c", 2, r128(I['c_2'], "o (t p) -> (o t) p", p=128), 8)
        for name, key, w in (("q_nope", 'q_nope_norm_w_2', 64), ("q_pe", 'q_pe_norm_w_2', 32),
                             ("k_nope", 'k_nope_norm_w_2', 64), ("k_pe", 'k_pe_norm_w_2', 32)):
            vec(name, 2, n=2, pieces=[((0, 2, c, c + w), I[key]) for c in range(0, 128, w)])
        for name, key in (("dt_bias", 'dt_bias_2'), ("a_log", 'a_log_2'), ("d_skip", 'd_skip_2')):
            vec(name, 2, n=2, pieces=[((0, 2, 32, 40), I[key])])
        e_vec = (s_vec, n_vec[0])
        e_if = misc_dma(invf, I['inv_freq'].rearrange("(p o) -> p o", o=1))

        b = bank()
        e = pe.trs([(b.ap[:, 128 * i:128 * i + 128], V[:, i, :], ident[:, :]) for i in range(3)], e_vec, e_id, e_on, e_Z, e_perm, e_tri, e_neg)
        e_VT = dve.copy(VT[:, :], b.ap[:, 0:384], e)
        e_vt_pe = e
        b.rel(e_VT)

        def col(name, i=0):
            return VT[:, vec_at[name] + i:vec_at[name] + i + 1]

        def cols(name, i, n):
            return VT[:, vec_at[name] + i:vec_at[name] + i + n]

        consts_ready = [None]
        e_c = act.f(c_act, cols("c", 0, 8), ACT.Silu, e_VT)
        lam = cols("lru_lambda", 0, 4)
        a0, a1, a2, a3 = (t8[i][:, 0:4] for i in range(4))
        e = act.f(a0, lam, ACT.Abs, e_VT)
        e = act.f(a1, a0, ACT.Exp, e, scale=-1.0)
        e = act.f(a2, a1, ACT.Ln, e, bias=1.0)
        e = dve.stt(a3, lam, 0.0, a2, MIN, SUB, e, e_VT)
        e_lam = dve.ts(clam, a3, 8.0, MUL, e)
        l0, l1 = cols("hgrn_lb_logits", 0, 8), cols("hgrn_lb_logits", 8, 8)
        e = dve.tt(t8[0], l0, l1, MAX, e_lam)
        e0 = dve.tt(t8[1], l0, t8[0], SUB, e)
        e1 = dve.tt(t8[2], l1, t8[0], SUB, e)
        e0 = act.f(t8[1], t8[1], ACT.Exp, e0)
        e1 = act.f(t8[2], t8[2], ACT.Exp, e1)
        e = dve.tt(t8[3], t8[1], t8[2], ADD, e0, e1)
        e = dve.recip(t8[4], t8[3], e)
        e0 = dve.tt(t8[1], t8[1], t8[4], MUL, e)
        e1 = dve.tt(t8[2], t8[2], t8[4], MUL, e)
        e = dve.tt(t8[3], t8[1], t8[2], ADD, e0, e1)
        e = dve.tt(t8[5], t8[3], t8[1], SUB, e)
        e1 = dve.ts(onelb, t8[5], -1.0, MUL, e, s2=1.0, op1=ADD)
        e0 = act.f(lnlb, t8[5], ACT.Ln, e)
        e1 = act.f(ln1lb, onelb, ACT.Ln, e1)
        e_lb = dve.tt(dif, ln1lb, lnlb, SUB, e0, e1)
        e = act.f(acol[32:40, :], cols("a_log", 0, 2)[32:40, :], ACT.Exp, e_VT)
        e_a = dve.ts(acol[32:40, :], acol[32:40, :], -1.0, MUL, e)
        def shares(dst, g, n, *ev):
            r = slice(32 * g, 32 * g + 32)
            return dve.copy(dst[r, 0:8 * n].rearrange("p (c n) -> p c n", n=n),
                            ident[r, 32 * g:32 * g + 8].unsqueeze(2).to_broadcast([32, 8, n]), *ev)

        e_X = shares(ar[:, 39, :], 1, 64, e_VT)
        b = bank()
        e = pe.mms([(b.ap[:, 4 * l + t:4 * l + t + 1],
                     ar[32:40, 39, 128 * t:128 * t + 128], col("d_skip", l)[32:40, :], True, True)
                    for l in range(2) for t in range(4)], e_X, b.free)
        e_X = e
        e_dsk = dve.copy(dskip, b.ap[:, 0:8], e)
        b.rel(e_dsk)
        consts_ready[0] = [e_c, e_lam, e_lb, e_a, e_dsk]

        xe, xrd = [None] * 8, [[] for _ in range(8)]
        st = {"hfree": [], "R": None, "Rrd": [], "sqf": [[], []], "accf": [], "T1f": [[], []], "T3f": [[], []],
              "afree": [e_vt_pe, e_X], "sfree": [], "hk": [None] * 8}

        for t in range(8):
            b = bank()
            e = pe.trs([(b.ap[:, 128 * k:128 * k + 128], xs_in[:, k, 128 * t:128 * t + 128], ident[:, :]) for k in range(4)],
                       (s_x, 64), b.free)
            xe[t] = act.f(x[:, t, :], b.ap[:, :], ACT.Copy, e)
            b.rel(xe[t])
            st["afree"] = [e, e_vt_pe, e_X]

        def square(t):
            if t == 0:
                e = act.f(acc[:, :], x[:, 0, :], ACT.Square, xe[0], st["accf"])
                st["acc"] = e
                return e
            i = t % 2
            e = act.f(sq[i][:, :], x[:, t, :], ACT.Square, xe[t], st["sqf"][i])
            st["acc"] = dve.tt(acc[:, :], acc[:, :], sq[i][:, :], ADD, e, st["acc"])
            st["sqf"][i] = [st["acc"]]
            return e

        def part(t, src, hi, lo, *ev):
            e1 = act.f(hi, src, ACT.Copy, *ev)
            e2 = dve.tt(lo, src, hi.bitcast(F32), SUB, e1, *ev)
            return [e1, e2]

        def norm_tile(t, gname, gi):
            g = col(gname, gi + t)
            e1 = act.f(hh[:, t, :], x[:, t, :], ACT.Copy, xe[t], st["hfree"], scale=g)
            e2 = dve.stt(hl[:, t, :], x[:, t, :], g, hh[:, t, :].bitcast(F32), MUL, SUB, e1)
            e3 = square(t)
            st["hk"][t] = [e1, e2]
            xrd[t] = [e1, e2, e3]

        def norm_end():
            b = bank()
            e = pe.mms([(b.ap[:, k:k + 1], acc[:, 128 * k:128 * k + 128], ones[:, 0:1], True, True) for k in range(4)],
                       st["acc"], b.free)
            st["accf"] = [e]
            e1 = dve.ts(tk, b.ap[:, 0:4], 1.0 / D, MUL, e, st.get("tkf"), s2=EPS, op1=ADD)
            b.rel(e1)
            e2 = pool.tt(rtok, tk, mhalf, ALU.pow, e1, e_mh, st["Rrd"])
            st["tkf"] = [e2]
            dg = sq[0][:, :].rearrange("p (b n) -> p b n", b=4)
            for k in range(4):
                e3 = dve.ts(dg[:, k, :], ident[:, :], rtok[:, k:k + 1], MUL, e2, st["sqf"][0])
            b = bank()
            e = pe.mms([(b.ap[:, 128 * k:128 * k + 128], ones[:, :], dg[:, k, :], True, True) for k in range(4)], e3, b.free)
            st["sqf"][0] = [e]
            e = act.f(R[:, :], b.ap[:, :], ACT.Copy, e, st["Rrd"])
            b.rel(e)
            st["R"] = e
            st["rtok"] = e2
            st["Rrd"] = []

        def norm_x(gname, gi):
            for t in range(8):
                norm_tile(t, gname, gi)
            norm_end()

        def modulated(nname, l, sc, sh):
            split(used[0] + SUBS - 1)
            ada_sums()
            norm_end()
            eG = dve.stt(G[:, :], mod[:, 48 * l + 8 * sc:48 * l + 8 * sc + 8], 1.0, cols(nname, 8 * l, 8), ADD, MUL,
                         mod_ev[0], st.get("Gf"))
            for t in range(8):
                i = t % 2
                e = dve.tt(T1[i][:, :], x[:, t, :], R[:, :], MUL, st["R"], st["T1f"][i], xe[t])
                e1 = act.f(T3[i][:, :], T1[i][:, :], ACT.Identity, e, eG, st["T3f"][i],
                           scale=G[:, t:t + 1], bias=mod[:, 48 * l + 8 * sh + t:48 * l + 8 * sh + t + 1])
                st["T1f"][i] = [e1]
                st["hk"][t] = part(t, T3[i][:, :], hh[:, t, :], hl[:, t, :], e1, st["hfree"])
                st["T3f"][i] = st["hk"][t]
                xrd[t] = [e]
            st["Rrd"] = [e]
            st["Gf"] = [e1]

        def after(nxt, t):
            if nxt is None:
                return
            if nxt[0] == "ffn":
                norm_tile(t, "ffn_norm", 16 * nxt[1] + 8 * nxt[2])
            elif nxt[0] in ("mix0", "mix1"):
                norm_tile(t, "mix_norm", 8 * (nxt[0] == "mix1"))
            elif nxt[0] == "ple":
                norm_tile(t, "ple_norm", 8 * nxt[1])
            else:
                xrd[t] = [square(t)]

        def deferred(nxt):
            return nxt is not None and nxt[0] in ("ffn", "mix0", "mix1", "ple")

        def enter(nxt):
            if nxt is None:
                return
            if deferred(nxt):
                norm_end()
            elif nxt[0] == "final":
                pass
            elif nxt[0] == "mix2":
                modulated("norm1", nxt[1], 1, 0)
            elif nxt[0] == "ffn2":
                modulated("norm2", nxt[1], 4, 3)

        def ffn(stage, nxt, scaled, scale, gate):
            key = stage
            wait_a = st["afree"]
            hid = [None] * FT
            for j in range(11):
                g1 = []
                for a in range(2):
                    b, e = product(key, hh, hl, st["hk"])
                    i = a
                    if scaled:
                        e = dve.tt(T1[i][:, :], b.ap[:, :], R[:, :], MUL, e, st["R"], st["T1f"][i])
                        b.rel(e)
                        e = act.f(T1[i][:, :], T1[i][:, :], ACT.Silu, e)
                    else:
                        e = act.f(T1[i][:, :], b.ap[:, :], ACT.Silu, e, st["T1f"][i])
                        b.rel(e)
                    g1.append(e)
                for a in range(2):
                    t = 2 * j + a
                    b, e = product(key, hh, hl, st["hk"])
                    i = a
                    if scaled:
                        e = dve.tt(T3[i][:, :], b.ap[:, :], R[:, :], MUL, e, st["R"], st["T3f"][i])
                        b.rel(e)
                        st["Rrd"] = [e]
                        e = dve.tt(T3[i][:, :], T3[i][:, :], T1[i][:, :], MUL, e, g1[a])
                    else:
                        e = dve.tt(T3[i][:, :], b.ap[:, :], T1[i][:, :], MUL, e, g1[a], st["T3f"][i])
                        b.rel(e)
                    st["T1f"][i] = [e]
                    hid[t] = part(t, T3[i][:, :], uh[:, t, :], ul[:, t, :], e, wait_a)
                    st["T3f"][i] = hid[t]
            st["hfree"] = [(pe.sem, pe.n)]
            for m in range(4):
                bs = [bank(), bank()]
                for k0, kt in ((0, 8), (8, 8), (16, 6)):
                    for a in range(2):
                        w = take(key)
                        pe.wait(w.ev, bs[a].free)
                        for k in range(kt):
                            e = pe.mms(three(bs[a].ap[:, :], w, k, C128, uh[:, k0 + k, :], ul[:, k0 + k, :],
                                             k0 + k == 0, k0 + k == FT - 1), hid[k0 + k])
                        give(w, e)
                        if k0 == 16:
                            t = 2 * m + a
                            xe[t] = dve.stt(x[:, t, :], bs[a].ap[:, :], gate(t) if gate else scale, x[:, t, :], MUL, ADD,
                                            e, xe[t], xrd[t])
                            bs[a].rel(xe[t])
                            after(nxt, t)
            st["afree"] = [(pe.sem, pe.n)]
            enter(nxt)

        def out_product(key, nxt, ev_k, gate=None):
            for t in range(8):
                b, e = product(key, ch, cl, ev_k)
                if gate:
                    xe[t] = dve.stt(x[:, t, :], b.ap[:, :], gate(t), x[:, t, :], MUL, ADD, e, xe[t], xrd[t])
                else:
                    xe[t] = dve.tt(x[:, t, :], b.ap[:, :], x[:, t, :], ADD, e, xe[t], xrd[t])
                b.rel(xe[t])
                after(nxt, t)
            st["afree"] = [(pe.sem, pe.n), (dve.sem, dve.n), (act.sem, act.n)]
            enter(nxt)

        def ple(stage, nxt):
            l = stage[1]
            praw = ar[:, 40:42, :].rearrange("p a n -> p (a n)").rearrange("p (b c) -> p b c", b=4)
            e_p = misc_dma(praw, I['p'][l, 0].rearrange("(b p) c -> p b c", p=128), st["afree"])
            pe_ev = []
            for k in range(8):
                b, e = product(stage, hh, hl, st["hk"])
                e = dve.tt(T1[k % 2][:, :], b.ap[:, :], R[:, :], MUL, e, st["R"], st["T1f"][k % 2])
                b.rel(e)
                st["Rrd"] = [e]
                e = act.f(A(16 + k), T1[k % 2][:, :], ACT.Sigmoid, e, st["afree"])
                st["T1f"][k % 2] = [e]
                pe_ev.append(e)
                if k == 3:
                    ek = []
                    for c in range(2):
                        b = bank()
                        e = pe.trs([(b.ap[:, 128 * j:128 * j + 128], praw[:, j, 128 * c:128 * c + 128], ident[:, :])
                                    for j in range(4)], e_p, b.free)
                        ek.append(part(c, b.ap[:, :], ch[:, c, :], cl[:, c, :], e, st["afree"]))
                        b.rel(ek[-1])
            st["hfree"] = [(pe.sem, pe.n)]
            for h in range(2):
                w = take(stage)
                for j in range(4):
                    t = 4 * h + j
                    b = bank()
                    its = []
                    for k in range(2):
                        its += three(b.ap[:, :], w, k, slice(128 * j, 128 * j + 128), ch[:, k, :], cl[:, k, :], k == 0, k == 1)
                    e = pe.mms(its, w.ev, b.free, ek)
                    give(w, e)
                    i = t % 2
                    e = dve.tt(T3[i][:, :], b.ap[:, :], A(16 + t), MUL, e, pe_ev[t], st["T3f"][i])
                    b.rel(e)
                    xe[t] = dve.tt(x[:, t, :], x[:, t, :], T3[i][:, :], ADD, e, xe[t], xrd[t])
                    st["T3f"][i] = [xe[t]]
                    after(nxt, t)
            st["afree"] = [(pe.sem, pe.n), (dve.sem, dve.n), (act.sem, act.n)]
            enter(nxt)

        def final(nxt):
            norm_end()
            for t in range(8):
                xe[t] = dve.stt(x[:, t, :], x[:, t, :], col("final_norm", t), R[:, :], MUL, MUL, st["R"], xe[t], xrd[t])
                st["Rrd"] = [xe[t]]
                after(nxt, t)
            enter(nxt)

        def conv(dst, src, w, b, *ev):
            e = dve.ts(dst, src, w(3), MUL, *ev, s2=b, op1=ADD)
            for s in range(1, 4):
                e = dve.stt(dst[:, s:S], src[:, 0:S - s], w(3 - s), dst[:, s:S], MUL, ADD, e)
            return e

        def row_stats(b, n, e):
            rr = sq[1]
            e1 = dve.ts(rr[0:n, :], b.ap[0:n, :], EPS, ADD, e, st["sqf"][1])
            b.rel(e1)
            e1 = act.f(rr[0:n, :], rr[0:n, :], ACT.Sqrt, e1)
            e1 = dve.recip(rr[0:n, :], rr[0:n, :], e1)
            st["sqf"][1] = [e1]
            return rr, e1

        def spread(rr, g, h, n, e, X=None):
            b = bank()
            l = ident[32 * g:32 * g + 32, 32 * g + h:32 * g + h + 1].to_broadcast([32, 128])
            if n > 1:
                l = X[32 * g:32 * g + 32, 128 // n * h:128 // n * h + 128]
            e = pe.mms([(b.ap[:, :], l, rr[32 * g:32 * g + 32, :], True, True)], e, b.free)
            st["sqf"][1] = [e]
            return b, e

        def chunk_mask(dst, n, *ev):
            e = pool.set(dst, 1.0, *ev)
            return pool.set(dst.rearrange("p (c n) -> p c n", n=n)[:, :, 0:1], 0.0, e)

        def mix0(stage, nxt):
            fr = st["afree"]
            hk = st["hk"]
            wbd = ar[:, 42:44, :].rearrange("p a (t n) -> p a t n", n=128)
            up = ar[0:16, 12, 0:256]
            e_z = pool.set(ar[:, 42:44, :], 0.0, fr)
            for a, n in enumerate(('lru_wa', 'lru_wx')):
                for h in range(2):
                    e_w = misc_dma(wbd[64 * h:64 * h + 64, a, :, 64 * h:64 * h + 64],
                                   I[n][0].rearrange("(t h) i j -> h i t j", h=2)[h], e_z)
            e_w = misc_dma(up, I['gla_gate_up'][0], fr)
            cm = A(13)
            e_cm = chunk_mask(cm, 64, fr)
            b, e = product(stage, hh, hl, hk)
            lrT = ar[0:16, 14, :]
            e_lr = dve.tt(lrT, b.ap[0:16, :], R[0:16, :], MUL, e, st["R"], fr)
            b.rel(e_lr)
            ek = []
            for j in range(2):
                b, e = product(stage, hh, hl, hk)
                e = dve.tt(A(18 + j), b.ap[:, :], R[:, :], MUL, e, fr)
                b.rel(e)
                ek.append(e)
            e_g, e_kd = [], []
            Gc = sm[:, 0:16].rearrange("p (j c) -> p j c", j=2)
            for j in range(2):
                b = bank()
                e = pe.mms([(b.ap[:, :], up[:, 128 * j:128 * j + 128], lrT, True, True)], e_lr, e_w, b.free)
                bi = col("gla_gate_bias", j)
                c = A(16 + j)
                w = A(j)
                e1 = act.f(w, b.ap[:, :], ACT.Abs, e, fr, bias=bi)
                e2 = dve.ts(c, b.ap[:, :], bi, ADD, e1, fr, s2=0.0, op1=MIN)
                b.rel(e2)
                e1 = act.f(w, w, ACT.Exp, e1, scale=-1.0)
                e1 = act.f(w, w, ACT.Ln, e1, bias=1.0)
                e = dve.tt(w, c, w, SUB, e1, e2)
                e = dve.scan(c, cm, w, e, e_cm)
                cv = c.rearrange("p (c n) -> p c n", n=64)
                wv = w.rearrange("p (c n) -> p c n", n=64)
                e1 = dve.tt(wv, cv[:, :, 63:64].to_broadcast([128, 8, 64]), cv, SUB, e)
                e_g.append(act.f(Gc[:, j, :], cv[:, :, 63], ACT.Exp, e, st.get("smf"), scale=1 / 16))
                e1 = act.f(w, w, ACT.Exp, e1, scale=1 / 16)
                e_kd.append(dve.tt(A(18 + j), A(18 + j), w, MUL, e1, ek[j]))
            eq = []
            for j in range(2):
                b, e = product(stage, hh, hl, hk)
                e = dve.stt(A(20 + j), b.ap[:, :], 0.125, R[:, :], MUL, MUL, e, fr)
                b.rel(e)
                eq.append(e)
            vt = A(22, 4)
            for t, (b, e) in enumerate(product_tok(stage, hh, hl, hk)):
                ev = dve.ts(vt[:, t, :], b.ap[:, :], rtok[:, t:t + 1], MUL, e, fr, st["rtok"])
                b.rel(ev)
            kdt = A(8, 2).rearrange("p a n -> p (a n)").rearrange("p (b n) -> p b n", b=4)
            sts = ar[:, 0:8, :]
            exc = []
            o_ev, kt_ev = [], []
            for t in range(4):
                b, e = product(stage, hh, hl, hk)
                e = dve.tt(A(30 + t), b.ap[:, :], R[:, :], MUL, e, fr)
                b.rel(e)
                exc.append(conv(A(34 + t), A(30 + t), lambda j: col("lru_conv_w", 4 * j + t), col("lru_conv_b", t), e, fr))
                if t < 2:
                    b = bank()
                    e = pe.trs([(b.ap[:, 128 * k:128 * k + 128], A(18 + t)[:, 128 * k:128 * k + 128], ident[:, :])
                                for k in range(4)], e_kd[t], b.free)
                    e = act.f(kdt[:, :, 128 * t:128 * t + 128], b.ap[:, :].rearrange("p (b n) -> p b n", b=4), ACT.Copy, e, fr)
                    b.rel(e)
                    kt_ev.append(e)
            es = None
            s_ev = []

            def state(c):
                nonlocal es
                b = bank()
                h = 64 * (c % 2)
                e = pe.mms([(b.ap[:, 256 * j:256 * j + 256], kdt[h:h + 64, c // 2, 128 * j:128 * j + 128],
                             vt[h:h + 64, c // 2, 256 * j:256 * j + 256], True, True) for j in range(2)], kt_ev, ev, b.free)
                if c == 0:
                    es = dve.copy(sts[:, 0, :], b.ap[:, :], e, e_kd)
                else:
                    p = es
                    for j in range(2):
                        r = slice(256 * j, 256 * j + 256)
                        es = dve.stt(sts[:, c, r], sts[:, c - 1, r], Gc[:, j, c:c + 1], b.ap[:, r], MUL, ADD, e, p, e_g[j])
                b.rel(es)
                s_ev.append(es)

            eg = []
            for t in range(4):
                b, e = product(stage, hh, hl, hk)
                e = dve.tt(A(26 + t), b.ap[:, :], R[:, :], MUL, e, fr)
                b.rel(e)
                eg.append(act.f(A(26 + t), A(26 + t), ACT.Silu, e))
                state(2 * t)
                state(2 * t + 1)
            er, ei = [], []
            exg = []
            for t in range(4):
                b, e = product(stage, hh, hl, hk)
                e = dve.tt(A(38 + t), b.ap[:, :], R[:, :], MUL, e, fr)
                b.rel(e)
                st["Rrd"] = [e]
                exg.append(act.f(A(38 + t), A(38 + t), ACT.Gelu_apprx_tanh, e))
            st["hfree"] = [(pe.sem, pe.n)]
            sfree = [(pe.sem, pe.n)]
            for t in range(4):
                for a, lst, dst, bn in ((0, er, 30, "lru_ba"), (1, ei, None, "lru_bx")):
                    b = bank()
                    e = pe.mms([(b.ap[:, :], wbd[:, a, t, :], A(34 + t), True, True)], exc[t], e_w, b.free)
                    d = A(30 + t) if a == 0 else sp[:, t, :]
                    e = act.f(d, b.ap[:, :], ACT.Sigmoid, e, exc[t], sfree, bias=col(bn, t))
                    b.rel(e)
                    lst.append(e)
            so = [sp[:, 4 + h, :] for h in range(4)]
            eo = []
            bs = None
            for h in range(4):
                b = bank()
                j, r = h // 2, 64 * (h % 2)
                e = pe.mms([(b.ap[:, 64 * c:64 * c + 64], sts[r:r + 64, c, 256 * j + 128 * (h % 2):256 * j + 128 * (h % 2) + 128],
                             A(20 + j)[r:r + 64, 64 * c:64 * c + 64], True, True) for c in range(8)], es, eq, b.free)
                e1 = dve.copy(so[h], b.ap[:, :], e, sfree)
                b.rel(e1)
                e2 = act.f(sp[:, 8 + h, :], so[h], ACT.Square, e1, sfree)
                eo.append(e1)
                if h == 0:
                    bs = bank()
                e3 = pe.mms([(bs.ap[0:32, :], Z["128"][:, 32 - h:64 - h], sp[:, 8 + h, :], h == 0, h == 3)], e2, bs.free)
            rr, e_rr = row_stats(bs, 32, e3)
            e_o_pe = e3
            ea, eu = [], []
            for t in range(4):
                e1 = act.f(sp[:, 12 + t, :], A(30 + t), ACT.Exp, er[t], sfree, scale=clam[:, t:t + 1])
                e2 = act.f(A(30 + t), A(30 + t), ACT.Tanh, er[t], scale=clam[:, t:t + 1])
                e3 = act.f(sp[:, 8 + t, :], sp[:, 12 + t, :], ACT.Square, e1, e_o_pe)
                e2 = dve.stt(A(30 + t), sp[:, 8 + t, :], 1.0, A(30 + t), ADD, MUL, e2, e3)
                e3 = dve.tt(sp[:, t, :], sp[:, t, :], A(34 + t), MUL, ei[t], exc[t])
                ea.append(e1)
                eu.append([e2, e3])
            ey = []
            for t in range(4):
                e = act.f(A(30 + t), A(30 + t), ACT.Sqrt, eu[t], scale=-1.0)
                e = dve.tt(sp[:, t, :], sp[:, t, :], A(30 + t), MUL, e, eu[t])
                e = dve.scan(A(34 + t), sp[:, 12 + t, :], sp[:, t, :], e, ea[t])
                e = dve.tt(A(38 + t), A(38 + t), A(34 + t), MUL, e, exg[t])
                ey.append(e)
            e_cat = [None] * 8
            free = [(pe.sem, pe.n)]
            for h in range(4):
                b, e = spread(rr, 0, h, 1, e_rr)
                e = dve.tt(so[h], so[h], b.ap[:, :], MUL, e, eo[h])
                b.rel(e)
                e = dve.stt(so[h], so[h], col("gla_head_norm"), A(26 + h), MUL, MUL, e, eg[h])
                e_cat[h] = part(h, so[h], ch[:, h, :], cl[:, h, :], e, free)
            for t in range(4):
                e_cat[4 + t] = part(t, A(38 + t), ch[:, 4 + t, :], cl[:, 4 + t, :], ey[t], free)
            st["hfree"] = [(pe.sem, pe.n), (dve.sem, dve.n), (act.sem, act.n)]
            st["smf"] = [(dve.sem, dve.n)]
            out_product(stage, nxt, e_cat)

        def mix1(stage, nxt):
            fr = st["afree"]
            hk = st["hk"]
            cm = sq[1][:, :]
            e_cm = chunk_mask(cm, 64, st["sqf"][1])
            Gc = ar[:, 43, 0:64].rearrange("p (h c) -> p h c", h=8)
            kdt = ar[:, 0:8, :].rearrange("p a n -> p (a n)").rearrange("p (b n) -> p b n", b=4)
            it = ar[:, 32:40, :].rearrange("p a n -> p (a n)").rearrange("p (b n) -> p b n", b=4)
            e_kd, e_g = [], []
            wf = [[], []]
            for t in range(8):
                b, e = product(stage, hh, hl, hk)
                z, kd, w = A(16 + t), A(24 + t), A(8 + t)
                e_z = dve.tt(z, b.ap[:, :], R[:, :], MUL, e, st["R"], fr)
                b.rel(e_z)
                e_k = act.f(kd, z, ACT.Sigmoid, e_z, fr, scale=-1.0)
                e = act.f(w, z, ACT.Abs, e_z, fr)
                e = act.f(w, w, ACT.Exp, e, scale=-1.0)
                e = act.f(w, w, ACT.Ln, e, bias=1.0)
                e_L = dve.stt(z, z, 0.0, w, MIN, SUB, e, e_k)
                e = act.f(w, z, ACT.Abs, e_L, bias=dif[:, t:t + 1])
                e = act.f(w, w, ACT.Exp, e, scale=-1.0)
                e = act.f(w, w, ACT.Ln, e, bias=1.0)
                e_m = dve.ts(z, z, ln1lb[:, t:t + 1], ADD, e, s2=lnlb[:, t:t + 1], op1=MAX)
                e = dve.tt(w, z, w, ADD, e_m, e)
                e = dve.scan(z, cm, w, e, e_cm)
                cv = z.rearrange("p (c n) -> p c n", n=64)
                wv = w.rearrange("p (c n) -> p c n", n=64)
                e1 = dve.tt(wv, cv[:, :, 63:64].to_broadcast([128, 8, 64]), cv, SUB, e)
                e_g.append(act.f(Gc[:, t, :], cv[:, :, 63], ACT.Exp, e, fr))
                e1 = act.f(w, w, ACT.Exp, e1)
                e_kd.append(dve.stt(kd, kd, onelb[:, t:t + 1], w, MUL, MUL, e1, e_k))
            st["sqf"][1] = [e_kd[7]]
            for s in range(2):
                for t, (b, e) in enumerate(product_tok(stage, hh, hl, hk)):
                    e_i = dve.ts(it[:, t, 512 * s:512 * s + 512], b.ap[:, :], rtok[:, t:t + 1], MUL, e, fr, st["rtok"])
                    b.rel(e_i)
            e_q, e_kt = [], []
            for t in range(8):
                b, e = product(stage, hh, hl, hk)
                e = dve.tt(A(16 + t), b.ap[:, :], R[:, :], MUL, e, e_kd[t], e_g[t])
                b.rel(e)
                e_q.append(act.f(A(16 + t), A(16 + t), ACT.Silu, e))
                b = bank()
                e = pe.trs([(b.ap[:, 128 * k:128 * k + 128], A(24 + t)[:, 128 * k:128 * k + 128], ident[:, :])
                            for k in range(4)], e_kd[t], b.free)
                e = dve.copy(kdt[:, :, 128 * t:128 * t + 128], b.ap[:, :].rearrange("p (b n) -> p b n", b=4), e, fr)
                b.rel(e)
                e_kt.append(e)
                e_tr = (pe.sem, pe.n)
            o_rd = [[], []]
            es = None

            def state(c):
                nonlocal es
                h0 = 64 * (c % 2)
                new = stt_buf[c % 2]
                old = stt_buf[(c + 1) % 2]
                p = es
                es = []
                for q in range(2):
                    b = bank()
                    e = pe.mms([(b.ap[:, 128 * i:128 * i + 128], kdt[h0:h0 + 64, c // 2, 128 * (4 * q + i):128 * (4 * q + i) + 128],
                                 it[h0:h0 + 64, c // 2, 128 * (4 * q + i):128 * (4 * q + i) + 128], True, True) for i in range(4)],
                               e_kt, e_i, b.free)
                    if c == 0:
                        e1 = dve.copy(new[q][:, :], b.ap[:, :], e, fr, st["T3f"][0])
                    else:
                        for i in range(4):
                            r = slice(128 * i, 128 * i + 128)
                            e1 = dve.stt(new[q][:, r], old[q][:, r], Gc[:, 4 * q + i, c:c + 1], b.ap[:, r], MUL, ADD,
                                         e, p, e_g, o_rd[c % 2])
                    b.rel(e1)
                    es.append(e1)
                b = bank()
                e = pe.mms([(b.ap[:, 64 * h:64 * h + 64], new[h // 4][:, 128 * (h % 4):128 * (h % 4) + 128],
                             A(16 + h)[:, 64 * c:64 * c + 64], True, True) for h in range(8)], es, e_q, b.free)
                o_rd[c % 2] = [e]
                e1 = dve.copy(ar[:, 24:32, 64 * c:64 * c + 64], b.ap[:, :].rearrange("p (h n) -> p h n", h=8), e, e_tr)
                b.rel(e1)
                return e1

            stt_buf = [[A(40), A(41)], [A(42), acc2]]
            e_gs = []
            for t in range(8):
                b, e = product(stage, hh, hl, hk)
                e = dve.tt(A(8 + t), b.ap[:, :], R[:, :], MUL, e, e_kd[t])
                b.rel(e)
                st["Rrd"] = [e]
                e_gs.append(act.f(A(8 + t), A(8 + t), ACT.Silu, e))
                e_o = state(t)
            st["hfree"] = [(pe.sem, pe.n)]
            st["T3f"][0] = [(pe.sem, pe.n), (dve.sem, dve.n)]
            sfree = [(pe.sem, pe.n)]
            bs = bank()
            for h in range(8):
                e2 = act.f(sp[:, h, :], A(24 + h), ACT.Square, e_o, sfree)
                e3 = pe.mms([(bs.ap[0:32, :], Z["128"][:, 32 - h:64 - h], sp[:, h, :], h == 0, h == 7)], e2, bs.free)
            rr, e_rr = row_stats(bs, 32, e3)
            e_cat = []
            free = [(pe.sem, pe.n)]
            for h in range(8):
                b, e = spread(rr, 0, h, 1, e_rr)
                e = dve.tt(A(24 + h), A(24 + h), b.ap[:, :], MUL, e, e_o, e2)
                b.rel(e)
                e = dve.stt(A(24 + h), A(24 + h), col("hgrn_head_norm"), A(8 + h), MUL, MUL, e, e_gs[h])
                e_cat.append(part(h, A(24 + h), ch[:, h, :], cl[:, h, :], e, free))
            st["hfree"] = [(pe.sem, pe.n), (dve.sem, dve.n), (act.sem, act.n)]
            out_product(stage, nxt, e_cat)

        acc2 = T3[0][:, :]

        def mix2(stage, nxt):
            l = stage[1]
            fr = st["afree"]
            hk = st["hk"]
            tok4 = "p (b n) -> p b n"
            co, si, an, tu = A(6), A(7), A(14), A(15)
            pos = tu.bitcast(I32)
            e = misc_dma(pos, I['positions_2'].to_broadcast([128, S]), fr)
            e = dve.copy(an, pos, e, fr)
            e = dve.ts(an, an, invf, MUL, e, e_if)
            MAGIC = 1.5 * 2.0 ** 23
            e1 = dve.ts(tu, an, 1 / (2 * np.pi), MUL, e, s2=MAGIC, op1=ADD)
            e1 = dve.ts(tu, tu, MAGIC, SUB, e1)
            c1 = 6.28125
            c2 = 2029 / 2.0 ** 20
            c3 = float(np.float32(2 * np.pi - c1 - c2))
            for cc in (c1, c2, c3):
                e1 = dve.stt(an, tu, -cc, an, MUL, ADD, e1)
            e1 = dve.ts(an, an, float(np.float32(3.1415925)), MIN, e1, s2=-float(np.float32(3.1415925)), op1=MAX)
            e_si = act.f(si, an, ACT.Sin, e1, fr)
            e = act.f(co, an, ACT.Sin, e1, fr, scale=0.5)
            e = act.f(co, co, ACT.Square, e)
            e_co = dve.ts(co, co, -2.0, MUL, e, s2=1.0, op1=ADD)
            cm = sq[0][:, :]
            X2, X4, two = A(11), A(3)[:, 0:256], A(3)[:, 256:512]
            for g in range(3):
                e_X = shares(X2, g, 64, fr)
            e_X = shares(X4, 1, 32, fr)
            for i, m in enumerate((ident, perm)):
                e_X = dve.copy(two[0:32, 128 * i:128 * i + 128].rearrange("p (a n) -> p a n", a=4),
                               m[0:32, 0:32].unsqueeze(1).to_broadcast([32, 4, 32]), fr)
            KP, QA, KA = A(38), [A(4), A(5)], A(12)
            bs = bank()
            b, e = product(stage, hh, hl, hk)
            e_kp = dve.copy(KP[0:32, :], b.ap[0:32, :], e, fr)
            e2 = act.f(T1[0][0:32, :], KP[0:32, :], ACT.Square, e_kp, st["T1f"][0])
            e2k = e2
            dt, ad, w8 = A(13), A(43), T3[0]
            bi = col("dt_bias", l)[32:40, :]
            e3 = act.f(w8[32:40, :], b.ap[32:40, :], ACT.Abs, e_kp, st["T3f"][0], bias=bi)
            e4 = dve.ts(dt[32:40, :], b.ap[32:40, :], bi, ADD, e3, fr, s2=0.0, op1=MAX)
            b.rel(e4)
            e3 = act.f(w8[32:40, :], w8[32:40, :], ACT.Exp, e3, scale=-1.0)
            e3 = act.f(w8[32:40, :], w8[32:40, :], ACT.Ln, e3, bias=1.0)
            e_dt = dve.tt(dt[32:40, :], dt[32:40, :], w8[32:40, :], ADD, e3, e4)
            st["T3f"][0] = [e_dt]
            e_cm = chunk_mask(cm, 128, st["sqf"][0])
            e = dve.ts(w8[32:40, :], dt[32:40, :], acol[32:40, l:l + 1], MUL, e_dt)
            e_ad = dve.scan(ad[32:40, :], cm[32:40, :], w8[32:40, :], e, e_cm, fr)
            st["T3f"][0] = [e_ad]
            st["sqf"][0] = [e_ad]
            e3 = pe.mms([(bs.ap[0:32, :], Z["k"][0:32, 30:62], T1[0][0:32, :], True, False)], e2, bs.free)
            st["T1f"][0] = [e3]
            e_qa = []
            for j in range(3):
                b, e = product(stage, hh, hl, hk)
                d = QA[j] if j < 2 else KA
                e1 = dve.copy(d, b.ap[:, :], e, fr)
                i = (j + 1) % 2
                b.rel(e1)
                e2 = act.f(T1[i][:, :], d, ACT.Square, e1, st["T1f"][i])
                zz = Z["256"][:, 32:64] if j < 2 else Z["128"][:, 31:63]
                e3 = pe.mms([(bs.ap[0:32, :], zz, T1[i][:, :], False, j == 2)], e2)
                st["T1f"][i] = [e3]
                e_qa.append([e1, e2])
            rr, e_rr = row_stats(bs, 32, e3)
            e_xb = []
            for t in range(8):
                b, e = product(stage, hh, hl, hk)
                i = t % 2
                e = act.f(T3[i][:, :], b.ap[:, :], ACT.Copy, e, st["T3f"][i])
                b.rel(e)
                e1 = conv(A(16 + t), T3[i][:, :], lambda j: col("conv_w", 32 * l + 8 * j + t), col("conv_b", 8 * l + t), e, fr)
                st["T3f"][i] = [e1]
                e_xb.append(act.f(A(16 + t), A(16 + t), ACT.Silu, e1))
                if t == 1:
                    e_n = []
                    for j in range(3):
                        b, e = spread(rr, 0, 0 if j < 2 else 1, 1, e_rr)
                        d = QA[j] if j < 2 else KA
                        wc = col("q_a", 2 * l + j) if j < 2 else col("kv_a", l)
                        e = dve.stt(d, d, wc, b.ap[:, :], MUL, MUL, e, e_qa[j])
                        b.rel(e)
                        e_n.append(part(j, d, ch[:, j, :], cl[:, j, :], e, fr))
                    b, e = spread(rr, 0, 2, 1, e_rr)
                    e = dve.stt(KP[0:32, :], KP[0:32, :], col("k_pe", l)[0:32, :], b.ap[0:32, :], MUL, MUL, e, e_kp, e2k)
                    b.rel(e)
                    e_kp = e
                if t == 3:
                    b1, b2 = bank(), bank()
                    e1 = pe.mms([(b1.ap[:, :], two[0:32, 0:128], KP[0:32, :], True, True),
                                 (b2.ap[:, :], two[0:32, 128:256], KP[0:32, :], True, True)],
                                e_kp, e_X, b1.free, b2.free)
                    e2 = dve.tt(A(14), b1.ap[:, :], co, MUL, e1, e_co)
                    b1.rel(e2)
                    e3 = dve.tt(A(15), b2.ap[:, :], si, MUL, e1, e_si)
                    b2.rel(e3)
                    e_kpe = dve.tt(KP, A(14), A(15), ADD, e2, e3)
            bs = bank()
            QN, QP, KN, vt = [A(28 + j) for j in range(4)], [A(32), A(33)], [A(34 + j) for j in range(4)], A(39, 4)
            e_q = {}
            pend = None

            def stat(rows, zz, src, e, start, stop):
                i = stat.n % 2
                stat.n += 1
                e2 = act.f(T1[i][:, :], src, ACT.Square, e, st["T1f"][i])
                e3 = pe.mms([(bs.ap[rows:rows + 32, :], zz, T1[i][:, :], start, stop)], e2, bs.free)
                st["T1f"][i] = [e3]
                return e2, e3

            stat.n = 0
            for s in range(2):
                w = take(stage)
                for m in range(3):
                    b = bank()
                    its = []
                    for k in range(2):
                        its += three(b.ap[:, :], w, k, slice(128 * m, 128 * m + 128), ch[:, k, :], cl[:, k, :], k == 0, k == 1)
                    e = pe.mms(its, w.ev, b.free, e_n[0], e_n[1])
                    give(w, e)
                    d = QN[2 * s + m] if m < 2 else QP[s]
                    e1 = dve.copy(d, b.ap[:, :], e, fr)
                    e2, e3 = stat(0 if m < 2 else 32,
                                  Z["64"][:, 32 - 2 * (2 * s + m):64 - 2 * (2 * s + m)] if m < 2 else Z["32"][:, 32 - 4 * s:64 - 4 * s],
                                  d, e1, s == 0 and m != 1, s == 1 and m != 0)
                    b.rel(e1)
                    e_q[(s, m)] = [e1, e2]
            w = take(stage)
            e_kn = []
            for j in range(4):
                b = bank()
                e = pe.mms(three(b.ap[:, :], w, 0, slice(128 * j, 128 * j + 128), ch[:, 2, :], cl[:, 2, :], True, True),
                           w.ev, b.free, e_n[2])
                e1 = dve.copy(KN[j], b.ap[:, :], e, fr)
                e2, e3 = stat(64, Z["64"][:, 32 - 2 * j:64 - 2 * j], KN[j], e1, j == 0, j == 3)
                b.rel(e1)
                e_kn.append([e1, e2])
            for k in range(4):
                b = bank()
                r = slice(128 * k, 128 * k + 128)
                e = pe.mms(three(b.ap[:, :], w, 0, slice(512, 1024), ch[:, 2, r], cl[:, 2, r], True, True, True),
                           w.ev, b.free, e_n[2])
                e_v = act.f(vt[:, k, :], b.ap[:, :], ACT.Copy, e, fr)
                b.rel(e_v)
            give(w, e)
            e_up = e
            rr, e_rr = row_stats(bs, 96, e3)
            e_zs = []
            for t in range(4):
                b, e = product(stage, hh, hl, hk)
                e_zs.append(act.f(A(24 + t), b.ap[:, :], ACT.Silu, e, fr))
                b.rel(e_zs[-1])
            st["hfree"] = [(pe.sem, pe.n)]
            sfree = [(pe.sem, pe.n)]
            e_QN, e_QP, e_KN = [], [], []
            for j in range(4):
                b, e = spread(rr, 0, 2 * j, 2, e_rr, X2)
                e = dve.stt(QN[j], QN[j], col("q_nope", l), b.ap[:, :], MUL, MUL, e, e_q[(j // 2, j % 2)])
                b.rel(e)
                e_QN.append(e)
                b, e = spread(rr, 2, 2 * j, 2, e_rr, X2)
                e = dve.stt(KN[j], KN[j], col("k_nope", l), b.ap[:, :], MUL, MUL, e, e_kn[j])
                b.rel(e)
                e_KN.append(e)
            for s in range(2):
                b, e = spread(rr, 1, 4 * s, 4, e_rr, X4)
                e = dve.stt(QP[s], QP[s], col("q_pe", l), b.ap[:, :], MUL, MUL, e, e_q[(s, 2)])
                b.rel(e)
                b = bank()
                e1 = pe.mms([(b.ap[:, :], perm[:, :], QP[s], True, True)], e, b.free)
                i = s
                e2 = dve.tt(T3[i][:, :], b.ap[:, :], si, MUL, e1, st["T3f"][i])
                b.rel(e2)
                e3 = dve.tt(QP[s], QP[s], co, MUL, e1)
                e3 = dve.tt(QP[s], QP[s], T3[i][:, :], ADD, e2, e3)
                st["T3f"][i] = [e3]
                e_QP.append(e3)
            SC = 96.0 ** -0.5
            P = [sp[:, 4 * i:4 * i + 4, :] for i in range(2)]
            PT = [sp[:, 8 + 4 * i:12 + 4 * i, :] for i in range(2)]
            mx = [t8[0], t8[1]]
            Pf, PTf, mxf = [sfree, sfree], [sfree, sfree], [[], []]
            e_cat = [None] * 8
            heads = {}

            def scores(h):
                i = h % 2
                j, r, g = h // 2, 64 * (h % 2), 32 * (h % 4)
                es = []
                for q in range(4):
                    b = bank()
                    n = 128 * q + 128
                    c = slice(128 * q, n)
                    e = pe.mms([(b.ap[:, 0:n], QN[j][r:r + 64, c], KN[j][r:r + 64, 0:n], True, False),
                                (b.ap[:, 0:n], QP[h // 4][g:g + 32, c], KP[g:g + 32, 0:n], False, False),
                                (b.ap[:, c], ident[:, :], neg[:, :], False, True)], e_QN, e_QP, e_KN, e_kpe, b.free)
                    m = mx[i]
                    e1 = dve.rmax(m[:, q:q + 1], b.ap[:, 0:n], e, mxf[i])
                    e1 = dve.ts(m[:, q:q + 1], m[:, q:q + 1], -SC, MUL, e1)
                    e2 = act.f(P[i][:, q, 0:n], b.ap[:, 0:n], ACT.Exp, e1, Pf[i], bias=m[:, q:q + 1], scale=SC,
                               accum_out=m[:, 4 + q:5 + q])
                    b.rel(e2)
                    es.append(e2)
                e1 = dve.recip(m[:, 4:8], m[:, 4:8], es)
                e3 = []
                for q in range(4):
                    e3.append(dve.ts(P[i][:, q, 0:128 * q + 128], P[i][:, q, 0:128 * q + 128], m[:, 4 + q:5 + q], MUL, e1))
                mxf[i] = [e3[3]]
                heads[h] = e3

            ob = [None]

            def values(h):
                i = h % 2
                e3 = heads[h]
                ep = []
                for k in range(4):
                    b = bank()
                    e = pe.trs([(b.ap[:, 128 * q:128 * q + 128], P[i][:, q, 128 * k:128 * k + 128], ident[:, :])
                                for q in range(k, 4)], e3, b.free)
                    fn = dve.copy if k % 2 else (lambda o, s, *ev: act.f(o, s, ACT.Copy, *ev))
                    ep.append(fn(PT[i][:, k, 128 * k:S], b.ap[:, 128 * k:S], e, PTf[i]))
                    b.rel(ep[-1])
                Pf[i] = [e]
                if h % 2 == 0:
                    ob[0] = bank()
                b = ob[0]
                r = 64 * (h % 2)
                e = pe.mms([(b.ap[r:r + 64, 128 * k:S], vt[:, k, 64 * h:64 * h + 64], PT[i][:, k, 128 * k:S], k == 0, k == 3)
                            for k in range(4)], ep, e_v, b.free)
                PTf[i] = [e]
                if h % 2:
                    e_cat[h // 2] = part(h, b.ap[:, :], ch[:, h // 2, :], cl[:, h // 2, :], e, e_up)
                    b.rel(e_cat[h // 2])

            for h in range(9):
                if h < 8:
                    scores(h)
                if h:
                    values(h - 1)
            done = [(pe.sem, pe.n), (act.sem, act.n), (dve.sem, dve.n)]
            X3 = T3[0][:, :]
            e_X = shares(X3, 1, 64, st["T3f"][0])
            b = bank()
            TKt = T1[0][:, 0:64].rearrange("p (a b h) -> p a b h", a=2, b=4)
            its = []
            for a, src in enumerate((dt, ad)):
                for k in range(4):
                    c = 32 * a + 8 * k
                    its.append((b.ap[:, c:c + 8], src[32:40, 128 * k:128 * k + 128], ident[32:40, 32:40]))
            e = pe.trs(its, e_dt, e_ad, b.free)
            e_tk = dve.copy(T1[0][:, 0:64], b.ap[:, 0:64], e, st["T1f"][0])
            b.rel(e_tk)
            al = T1[1][:, 0:32].rearrange("p (b h) -> p b h", b=4)
            cd = T1[1][:, 32:64].rearrange("p (b h) -> p b h", b=4)
            de = T1[1][:, 64:96].rearrange("p (b h) -> p b h", b=4)
            W = [sp[:, h, :].rearrange(tok4, b=4) for h in range(8)]
            Gm = [A(38), A(39)]
            e_gm = []
            for g in range(2):
                b = bank()
                e = pe.mms([(b.ap[:, 128 * k:128 * k + 128], A(20 + g)[:, 128 * k:128 * k + 128],
                             A(22 + g)[:, 128 * k:128 * k + 128], True, True) for k in range(4)], e_xb, b.free)
                e = dve.tt(Gm[g].rearrange(tok4, b=4), b.ap[:, :].rearrange(tok4, b=4),
                           tri[:, :].unsqueeze(1).to_broadcast([128, 4, 128]), MUL, e, done)
                b.rel(e)
                e_gm.append(e)
            e_W, e_al = [], None
            for h in range(8):
                b = bank()
                e = pe.mms([(b.ap[:, :], ident[32:40, 32 + h:33 + h].to_broadcast([8, 128]), ad[32:40, :], True, True)], e_ad, b.free)
                bv = b.ap[:, :].rearrange(tok4, b=4)
                e_al = dve.copy(al[:, :, h:h + 1], bv[:, :, 127:128], e, st["T1f"][1])
                for k in range(4):
                    e1 = dve.ts(W[h][:, k, :], bv[:, k, :], TKt[:, 1, k, h:h + 1], SUB, e, e_tk, done, s2=0.0, op1=MIN)
                b.rel(e_al, e1)
                e1 = act.f(sp[:, h, :], sp[:, h, :], ACT.Exp, e1)
                e_W.append(dve.tt(sp[:, h, :], sp[:, h, :], Gm[h // 4], MUL, e1, e_gm[h // 4]))
            e1 = act.f(cd, al, ACT.Exp, e_al)
            e2 = dve.tt(de, al, TKt[:, 1], SUB, e_al, e_tk)
            e_de = act.f(de, de, ACT.Exp, e2)
            e_cd = e1
            xt, xd = A(28, 4), A(32, 4)
            Bt = A(36, 2).rearrange("p g (b n) -> p g b n", b=4)
            e_xt, e_xd, e_bt = [], [], []
            for t in range(4):
                b = bank()
                e = pe.trs([(b.ap[:, 128 * k:128 * k + 128], A(16 + t)[:, 128 * k:128 * k + 128], ident[:, :]) for k in range(4)],
                           e_xb, b.free)
                o = xt[:, :, 128 * t:128 * t + 128].rearrange("p b (h n) -> p b h n", h=2)
                e = dve.tt(o, b.ap[:, :].rearrange("p (b h n) -> p b h n", b=4, h=2),
                           TKt[:, 0, :, 2 * t:2 * t + 2].unsqueeze(3).to_broadcast([128, 4, 2, 64]), MUL, e, e_tk, done)
                b.rel(e)
                e_xt.append(e)
                e_xd.append(dve.tt(xd[:, :, 128 * t:128 * t + 128].rearrange("p b (h n) -> p b h n", h=2), o,
                                   de[:, :, 2 * t:2 * t + 2].unsqueeze(3).to_broadcast([128, 4, 2, 64]), MUL, e, e_de, done))
            for g in range(2):
                b = bank()
                e = pe.trs([(b.ap[:, 128 * k:128 * k + 128], A(20 + g)[:, 128 * k:128 * k + 128], ident[:, :]) for k in range(4)],
                           e_xb, b.free)
                e_bt.append(act.f(A(36 + g), b.ap[:, :], ACT.Copy, e, done))
                b.rel(e_bt[-1])
            PV = [None, A(40), A(41), A(42)]
            e_pv = [None]
            for c in range(3):
                b = bank()
                e = pe.mms([(b.ap[:, 256 * g:256 * g + 256], Bt[:, g, c, :], xd[:, c, 256 * g:256 * g + 256], True, True)
                            for g in range(2)], e_bt, e_xd, b.free)
                if c == 0:
                    e1 = dve.copy(PV[1], b.ap[:, :], e, done)
                else:
                    o = PV[c + 1].rearrange("p (h n) -> p h n", h=8)
                    e1 = dve.tt(o, PV[c].rearrange("p (h n) -> p h n", h=8), cd[:, c, :].unsqueeze(2).to_broadcast([128, 8, 64]),
                                MUL, e_pv[c], e_cd, done)
                    e1 = dve.tt(PV[c + 1], PV[c + 1], b.ap[:, :], ADD, e1, e)
                b.rel(e1)
                e_pv.append(e1)
            bs = bank()
            e_y = []
            for t in range(4):
                b = bank()
                e = pe.mms([(b.ap[:, :], X3[32:40, 128 * t:128 * t + 128], ad[32:40, :], True, True)], e_ad, e_X, b.free)
                st["T3f"][0] = [e]
                E = sp[:, 8 + t, :]
                e_E = act.f(E, b.ap[:, :], ACT.Exp, e, done)
                b.rel(e_E)
                y = sp[:, 12 + t, :]
                b = bank()
                e = pe.mms([(b.ap[64 * h:64 * h + 64, 128 * c:128 * c + 128], xt[:, c, 128 * t + 64 * h:128 * t + 64 * h + 64],
                             W[2 * t + h][:, c, :], True, True) for c in range(4) for h in range(2)],
                           e_xt, e_W[2 * t], e_W[2 * t + 1], b.free)
                e = dve.stt(y, A(16 + t), dskip[:, 4 * l + t:4 * l + t + 1], b.ap[:, :], MUL, ADD, e, done, e_xb[t])
                b.rel(e)
                b = bank()
                e1 = pe.mms([(b.ap[:, 128 * c:128 * c + 128], PV[c][:, 128 * t:128 * t + 128],
                              A(22 + t // 2)[:, 128 * c:128 * c + 128], True, True) for c in range(1, 4)], e_pv[3], b.free)
                e1 = dve.tt(E[:, 128:S], E[:, 128:S], b.ap[:, 128:S], MUL, e1, e_E)
                b.rel(e1)
                e = dve.tt(y[:, 128:S], y[:, 128:S], E[:, 128:S], ADD, e, e1)
                e = dve.tt(y, y, A(24 + t), MUL, e, e_zs[t])
                e2 = act.f(E, y, ACT.Square, e, e1)
                e3 = pe.mms([(bs.ap[0:32, :], Z["256"][:, 32 - t // 2:64 - t // 2], E, t == 0, t == 3)], e2, bs.free)
                e_y.append(e)
            st["T1f"] = [[(dve.sem, dve.n)], [(dve.sem, dve.n)]]
            rr, e_rr = row_stats(bs, 32, e3)
            for g in range(2):
                b, e = spread(rr, 0, g, 1, e_rr)
                for t in (2 * g, 2 * g + 1):
                    y = sp[:, 12 + t, :]
                    e1 = dve.stt(y, y, col("ssd_norm", 4 * l + t), b.ap[:, :], MUL, MUL, e, e_y[t])
                    e_cat[4 + t] = part(t, y, ch[:, 4 + t, :], cl[:, 4 + t, :], e1, done)
                b.rel(e1)
            st["hfree"] = [(pe.sem, pe.n), (dve.sem, dve.n), (act.sem, act.n)]
            out_product(stage, nxt, e_cat, lambda t: mod[:, 48 * l + 16 + t:48 * l + 17 + t])

        def first(stage):
            for t in range(8):
                after(stage, t)
            enter(stage)

        first(stages[0])
        for i, stage in enumerate(stages):
            nxt = stages[i + 1] if i + 1 < len(stages) else None
            if stage[0] == "ffn":
                ffn(stage, nxt, True, 0.5, None)
            elif stage[0] == "ffn2":
                ffn(stage, nxt, False, None, lambda t, l=stage[1]: mod[:, 48 * l + 40 + t:48 * l + 41 + t])
            elif stage[0] == "mix0":
                mix0(stage, nxt)
            elif stage[0] == "mix1":
                mix1(stage, nxt)
            elif stage[0] == "ple":
                ple(stage, nxt)
            elif stage[0] == "final":
                final(nxt)
            elif stage[0] == "mix2":
                mix2(stage, nxt)

        od = out[0].rearrange("(b p) d -> p b d", p=128)
        for k in range(4):
            for h in range(2):
                b = bank()
                e = pe.trs([(b.ap[:, 128 * j:128 * j + 128], x[:, 4 * h + j, 128 * k:128 * k + 128], ident[:, :])
                            for j in range(4)], xe, b.free)
                d = A(2 * k + h)
                e = act.f(d, b.ap[:, :], ACT.Copy, e, st["afree"]) if h else dve.copy(d, b.ap[:, :], e, st["afree"])
                b.rel(e)
                sp_q.dma(lambda q, d=d, k=k, h=h: q.dma_start(od[:, k, 512 * h:512 * h + 512], d), s_out, e)
        sp_q.wait((s_out, 16 * 8), (s_misc, misc[0]))

        block = ctx.enter_context(nc.Block())
        block.sync(lambda e: sp_q.run(e))
        block.scalar(lambda e: act.run(e))
        block.vector(lambda e: dve.run(e))
        block.gpsimd(lambda e: pool.run(e))
        block.tensor(lambda e: pe.run(e))


def kernel(**inputs):
    import concourse.bacc as _bacc
    from concourse.bass_utils import run_bass_kernel_spmd as _run

    inv = np.float32(1.0) / np.power(np.float32(10000.0), np.arange(0, 32, 2, dtype=np.float32) / np.float32(32))
    inputs = dict(inputs, inv_freq=np.tile(inv.astype(np.float32), 8))
    nc = _bacc.Bacc("TRN2", target_bir_lowering=False, num_devices=1)
    arrays, aps = {}, {}
    for name in INS:
        a = np.ascontiguousarray(inputs[name])
        arrays[f"in_{name}"] = a
        aps[name] = nc.dram_tensor(f"in_{name}", a.shape, mybir.dt.from_np(a.dtype), kind="ExternalInput").ap()
    out = nc.dram_tensor("out_0", (1, S, D), F32, kind="ExternalOutput").ap()
    build(nc, aps, out, STAGES)
    r = _run(nc, [arrays], core_ids=[0])
    return r.results[0]["out_0"]
```

```python
import numpy as np
from contextlib import ExitStack

import concourse.bass as bass
from concourse import mybir

F32 = mybir.dt.float32
F32R = mybir.dt.float32r
I32 = mybir.dt.int32
ALU = mybir.AluOpType
ACT = mybir.ActivationFunctionType
AX = mybir.AxisListType
MUL, ADD, SUB, MAX, MIN = ALU.mult, ALU.add, ALU.subtract, ALU.max, ALU.min

D, S, NF, FT, EPS = 1024, 512, 2816, 22, 1e-6
RAW, SUBS = 3, 3


class Queue:

    def __init__(self, sem):
        self.sem, self.n, self.ops, self.seen = sem, 0, [], {}

    def wait(self, *events):
        for e in events:
            if e is None:
                continue
            if isinstance(e, list):
                self.wait(*e)
                continue
            sem, v = e
            if self.seen.get(sem.name, 0) < v:
                self.seen[sem.name] = v
                self.ops.append((None, sem, v))

    def do(self, fn, *events):
        self.wait(*events)
        self.n += 1
        self.ops.append((fn, self.sem, 1))
        return self.sem, self.n

    def dma(self, fn, sem, *events):
        self.wait(*events)
        self.ops.append((fn, sem, 16))

    def quiet(self, fn):
        self.ops.append((fn, None, 0))

    def run(self, eng):
        for fn, sem, v in self.ops:
            if fn is None:
                eng.wait_ge(sem, v)
            elif sem is None:
                fn(eng)
            else:
                fn(eng).then_inc(sem, v)


class Act(Queue):
    def f(self, out, in_, func, *ev, **kw):
        return self.do(lambda e: e.activation(out, in_, func, **kw), *ev)


class Alu(Queue):
    def tt(self, out, a, b, op, *ev):
        return self.do(lambda e: e.tensor_tensor(out, a, b, op), *ev)

    def ts(self, out, a, s1, op0, *ev, s2=None, op1=None):
        if op1 is None:
            return self.do(lambda e: e.tensor_scalar(out, a, s1, None, op0), *ev)
        return self.do(lambda e: e.tensor_scalar(out, a, s1, s2, op0, op1), *ev)

    def stt(self, out, a, s, b, op0, op1, *ev):
        return self.do(lambda e: e.scalar_tensor_tensor(out=out, in0=a, scalar=s, in1=b, op0=op0, op1=op1), *ev)

    def copy(self, out, a, *ev):
        return self.do(lambda e: e.tensor_copy(out, a), *ev)

    def recip(self, out, a, *ev):
        return self.do(lambda e: e.reciprocal(out, a), *ev)

    def scan(self, out, m, a, *ev):
        return self.do(lambda e: e.tensor_tensor_scan(out, m, a, 0.0, MUL, ADD), *ev)

    def rmax(self, out, a, *ev):
        return self.do(lambda e: e.tensor_reduce(out, a, AX.X, MAX), *ev)

    def set(self, out, v, *ev):
        return self.do(lambda e: e.memset(out, v), *ev)

    def select(self, out, pattern, base, mult, op, fill, *ev):
        return self.do(lambda e: e.affine_select(out=out, in_=out, compare_op=op, fill=fill, base=base,
                                                 pattern=pattern, channel_multiplier=mult), *ev)


class Pe(Queue):
    def mms(self, items, *ev):
        self.wait(*ev)
        for it in items[:-1]:
            self.quiet(self.one(it))
        return self.do(self.one(items[-1]))

    @staticmethod
    def one(it):
        out, l, r, a, z = it
        return lambda e: e.matmul(out, l, r, start=a, stop=z, skip_group_check=True)

    def trs(self, items, *ev):
        self.wait(*ev)
        for o, i, d in items[:-1]:
            self.quiet(lambda e, o=o, i=i, d=d: e.transpose(o, i, d))
        o, i, d = items[-1]
        return self.do(lambda e: e.transpose(o, i, d))


class Bank:
    def __init__(self, ap):
        self.ap, self.free, self.busy = ap, [], False

    def rel(self, *ev):
        self.free, self.busy = list(ev), False


class Sub:
    pass


INS = ['x', 'p', 'ffn_norm', 'ffn_w1', 'ffn_w3', 'ffn_w2', 'mix_norm', 'ple_norm', 'ple_proj', 'ple_gate',
       'final_norm', 'm0_w_in', 'gla_gate_up', 'gla_gate_bias', 'gla_head_norm', 'lru_conv_w', 'lru_conv_b',
       'lru_wa', 'lru_ba', 'lru_wx', 'lru_bx', 'lru_lambda', 'm0_w_out', 'm1_w_in', 'hgrn_lb_logits',
       'hgrn_head_norm', 'm1_w_out', 'c_2', 'positions_2', 'norm1_w_2', 'norm2_w_2', 'w_ada_2', 'b_ada_2',
       'w_in_2', 'q_a_norm_w_2', 'w_q_up_2', 'kv_a_norm_w_2', 'w_kv_up_2', 'q_nope_norm_w_2',
       'q_pe_norm_w_2', 'k_nope_norm_w_2', 'k_pe_norm_w_2', 'conv_w_2', 'conv_b_2', 'dt_bias_2', 'a_log_2',
       'd_skip_2', 'ssd_norm_w_2', 'w_out_2', 'w_gate_up_2', 'w_down_2', 'inv_freq']

STAGES = [("ffn", 0, 0), ("mix0",), ("ffn", 0, 1), ("ple", 0), ("ffn", 1, 0), ("mix1",), ("ffn", 1, 1),
          ("ple", 1), ("final",), ("mix2", 0), ("ffn2", 0), ("mix2", 1), ("ffn2", 1)]
ADA_PER_FFN = 12


def build(nc, I, out, stages):
    ctx = ExitStack()
    with ctx:
        def sem(name):
            return ctx.enter_context(nc.semaphore(name))

        off = [nc.sbuf_base + (-nc.sbuf_base) % 64]

        def sb(name, shape, dt=F32, alias=None):
            n = 4 * int(np.prod(shape[1:]))
            o = off[0] if alias is None else alias
            if alias is None:
                off[0] += n + (-n) % 32
            t = place(name, shape, dt, o)
            return t, o

        def place(name, shape, dt, o):
            return nc.alloc_sbuf_tensor_at(name, shape, dt, offset=o)

        x, _ = sb("x", [128, 8, S])
        hh, o_h = sb("hh", [128, 8, S], F32R)
        hl, o_l = sb("hl", [128, 8, S], F32R)
        sp, _ = sb("sp", [128, 16, S], F32, o_h)
        ar, o_a = sb("ar", [128, 2 * FT, S])
        uh, _ = sb("uh", [128, FT, S], F32R, o_a)
        ul, _ = sb("ul", [128, FT, S], F32R, o_a + FT * S * 4)
        ch, _ = sb("ch", [128, 8, S], F32R, o_a)
        cl, _ = sb("cl", [128, 8, S], F32R, o_a + 8 * S * 4)
        raw = [sb(f"raw{i}", [128, 2048])[0] for i in range(RAW)]
        wh = [sb(f"wh{i}", [128, 1024], F32R)[0] for i in range(SUBS)]
        wl = [sb(f"wl{i}", [128, 1024], F32R)[0] for i in range(SUBS)]
        VT, _ = sb("VT", [128, 3 * 128])
        ident, _ = sb("ident", [128, 128])
        ones, _ = sb("ones", [128, 128])
        tri, _ = sb("tri", [128, 128])
        neg, _ = sb("neg", [128, 128])
        perm, _ = sb("perm", [128, 128])
        Z = {n: sb(f"Z{n}", [128, 64])[0] for n in ("256", "128", "64", "32", "k")}
        R, _ = sb("R", [128, S])
        sq = [sb(f"sq{i}", [128, S])[0] for i in range(2)]
        acc, _ = sb("acc", [128, S])
        T1 = [sb(f"T1{i}", [128, S])[0] for i in range(2)]
        T3 = [sb(f"T3{i}", [128, S])[0] for i in range(2)]
        ada = [sb("ada", [128, 256])[0]]
        mod, _ = sb("mod", [128, 96])
        G, _ = sb("G", [128, 8])
        small, _ = sb("small", [128, 160])
        assert off[0] <= nc.sbuf_top, (off[0], nc.sbuf_top)

        psum = [ctx.enter_context(nc.psum_tensor(f"ps{i}", [128, S], F32)) for i in range(8)]

        act, dve, pool, pe, sp_q = (C(sem(n)) for C, n in
                                    ((Act, "s_act"), (Alu, "s_dve"), (Alu, "s_pool"), (Pe, "s_pe"), (Queue, "s_sp")))
        s_raw = [sem(f"s_raw{i}") for i in range(RAW)]
        s_vec, s_x, s_misc, s_out = sem("s_vec"), sem("s_x"), sem("s_misc"), sem("s_out")
        misc = [0]

        def A(i, n=1):
            return ar[:, i, :] if n == 1 else ar[:, i:i + n, :]

        def misc_dma(dst, src, *ev):
            act.dma(lambda e: e.dma_start(dst, src), s_misc, *ev)
            misc[0] += 16
            return s_misc, misc[0]

        banks = [Bank(p) for p in psum]
        turn = [0]

        def bank():
            for _ in range(8):
                b = banks[turn[0] % 8]
                turn[0] += 1
                if not b.busy:
                    b.busy = True
                    return b
            raise AssertionError("no bank")

        chunks, subs = [], []

        def chunk(key, kt, width, pieces, parts, kind="mm"):
            n = len(chunks)
            chunks.append((kt, width, pieces, len(parts)))
            for i, pt in enumerate(parts):
                subs.append((key, n, *pt, *((0, kt) if len(pt) == 2 else ()), kind, i == len(parts) - 1))

        def wide(key, W, c0, n, k0=0, kt=8):
            for c in range(0, n, 256):
                w = min(256, n - c)
                chunk(key, kt, w, [(0, W[k0:k0 + kt * 128, c0 + c:c0 + c + w])],
                      [(i, 128) for i in range(0, w, 128)])

        def tall(key, W, c0, n):
            for c in range(c0, c0 + n, 512):
                for k in range(2):
                    chunk(key, 4, 512, [(0, W[512 * k:512 * k + 512, c:c + 512])], [(0, 512, 0, 2), (0, 512, 2, 2)])

        ada_next = [0]

        def plan_ada(n):
            for _ in range(n):
                i = ada_next[0]
                if i < 48:
                    l, c = divmod(i, 24)
                    chunk(("ada", i), 8, 256, [(0, I['w_ada_2'][l][:, c * 256:c * 256 + 256])], [(0, 256)], "ada")
                    ada_next[0] += 1

        def plan_ffn(key, w1, w3, w2, with_ada):
            for j in range(11):
                wide(key, w1, j * 256, 256)
                wide(key, w3, j * 256, 256)
                if with_ada:
                    plan_ada(1)
            for m in range(4):
                for k0, kt in ((0, 8), (8, 8), (16, 6)):
                    wide(key, w2, m * 256, 256, k0 * 128, kt)
                if with_ada and m == 1:
                    plan_ada(ADA_PER_FFN - 11)

        for st in stages:
            if st[0] == "ffn":
                plan_ffn(st, I['ffn_w1'][st[1], st[2]], I['ffn_w3'][st[1], st[2]], I['ffn_w2'][st[1], st[2]], True)
            elif st[0] == "mix0":
                W = I['m0_w_in'][0]
                for c, n in ((1536, 128), (256, 256), (1552, 512), (0, 256)):
                    wide(st, W, c, n)
                tall(st, W, 512, 512)
                for c in (1024, 2064):
                    wide(st, W, c, 512)
                wide(st, I['m0_w_out'][0], 0, 1024)
            elif st[0] == "mix1":
                W = I['m1_w_in'][0]
                wide(st, W, 1024, 1024)
                tall(st, W, 2048, 1024)
                wide(st, W, 0, 1024)
                wide(st, W, 3072, 1024)
                wide(st, I['m1_w_out'][0], 0, 1024)
            elif st[0] == "ple":
                wide(st, I['ple_gate'][st[1]], 0, 1024)
                chunk(st, 2, 1024, [(0, I['ple_proj'][st[1]])], [(0, 512), (512, 512)])
            elif st[0] == "mix2":
                l = st[1]
                W = I['w_in_2'][l]
                plan_ada(48 - ada_next[0])
                chunk(st, 8, 128, [(0, W[:, 384:416]), (32, W[:, 1952:1960]), (40, W[:, 416:504])], [(0, 128)])
                wide(st, W, 0, 256)
                wide(st, W, 256, 128)
                wide(st, W, 928, 512)
                Wq = I['w_q_up_2'][l].rearrange("k (h n) -> k h n", n=96)
                chunk(st, 2, 768, [(384 * s + c, Wq[:, 4 * s:4 * s + 4, a:z]) for s in range(2)
                                   for c, a, z in ((0, 0, 64), (256, 64, 96))], [(0, 384), (384, 384)])
                Wk = I['w_kv_up_2'][l].rearrange("k (h n) -> k h n", n=128)
                chunk(st, 1, 1024, [(0, Wk[:, :, 0:64]), (512, Wk[:, :, 64:128])], [(0, 1024)])
                wide(st, W, 1440, 512)
                wide(st, W, 416, 512)
                wide(st, I['w_out_2'][l], 0, 1024)
            elif st[0] == "ffn2":
                l = st[1]
                W = I['w_gate_up_2'][l]
                plan_ffn(st, W[:, 0:NF], W[:, NF:2 * NF], I['w_down_2'][l], False)
        if any(st[0] == "mix2" for st in stages):
            assert ada_next[0] == 48

        raw_free = [[] for _ in range(RAW)]
        raw_n = [0] * RAW
        raw_ev = {}
        sent = [0]

        def send():
            n = sent[0]
            if n >= len(chunks):
                return
            sent[0] += 1
            kt, width, pieces, _ = chunks[n]
            s = n % RAW
            v = raw[s][:, 0:kt * width].rearrange("p (t n) -> p t n", t=kt)
            sp_q.wait(raw_free[s])
            for c, src in pieces:
                if len(src.shape) == 2:
                    moves = [(v[:, :, c:c + src.shape[1]], src.rearrange("(t p) n -> p t n", p=128))]
                else:
                    w, n_h = src.shape[1] * src.shape[2], src.shape[2]
                    moves = [(v[:, t, c:c + w].rearrange("p (h n) -> p h n", n=n_h), src[128 * t:128 * t + 128])
                             for t in range(kt)]
                for d, r in moves:
                    sp_q.dma(lambda e, d=d, r=r: e.dma_start(d, r), s_raw[s])
                    raw_n[s] += 16
            raw_ev[n] = (s_raw[s], raw_n[s])

        sub_free = [[] for _ in range(SUBS)]
        ready = {}
        done_subs = [0, 0]
        ada_free = [[]]
        ada_wait = []
        mod_ev = [None]

        def split(limit):
            while done_subs[0] < len(subs):
                key, n, c, w, t0, tn, kind, last = subs[done_subs[0]]
                if kind == "mm" and done_subs[1] > limit:
                    return
                if kind == "ada" and consts_ready[0] is None:
                    return
                done_subs[0] += 1
                kt, width, _, _ = chunks[n]
                src = raw[n % RAW][:, 0:kt * width].rearrange("p (t n) -> p t n", t=kt)[:, t0:t0 + tn, c:c + w]
                if kind == "mm":
                    g = done_subs[1]
                    done_subs[1] += 1
                    s = g % SUBS
                    hi = wh[s][:, 0:tn * w].rearrange("p (t n) -> p t n", t=tn)
                    lo = wl[s][:, 0:tn * w].rearrange("p (t n) -> p t n", t=tn)
                    e1 = act.f(hi, src, ACT.Copy, raw_ev[n], sub_free[s])
                    e2 = dve.tt(lo, src, hi.bitcast(F32), SUB, e1)
                    t = Sub()
                    t.key, t.hi, t.lo, t.ev, t.slot, t.kt = key, hi, lo, [e1, e2], s, tn
                    ready[g] = t
                    e = [e1, e2]
                else:
                    ada_sums()
                    i = key[1]
                    a = ada[0]
                    e = dve.ts(a[:, :], src[:, 0, :], c_act[:, 0:1], MUL, raw_ev[n], ada_free[0], consts_ready[0])
                    for t in range(1, 8):
                        e = dve.stt(a[:, :], src[:, t, :], c_act[:, t:t + 1], a[:, :], MUL, ADD, e)
                    ada_wait.append((i, a, e, used[0]))
                    e = [e]
                if last:
                    raw_free[n % RAW] = e
                    send()

        def ada_sums(late=0):
            while ada_wait and ada_wait[0][3] + late <= used[0]:
                i, a, e, _ = ada_wait.pop(0)
                b = bank()
                e = pe.mms([(b.ap[:, h:h + 1], a[:, 128 * h:128 * h + 128], one, True, True)
                            for h in range(2)], e, b.free)
                ada_free[0] = [e]
                mod_ev[0] = dve.tt(mod[:, 2 * i:2 * i + 2], b.ap[:, 0:2], VT[:, vec_at["b_ada"] + 2 * i:vec_at["b_ada"] + 2 * i + 2], ADD, e)
                b.rel(mod_ev[0])

        used = [0]
        side = []

        def advance():
            for c in list(side):
                if next(c, 0) == 0 and c in side:
                    side.remove(c)

        def beside(chain):
            side.append(chain)
            return chain

        def finish(chain):
            while chain in side:
                advance()

        def take(key, ahead=SUBS - 1):
            g = used[0]
            used[0] += 1
            ada_sums(2)
            split(g + ahead)
            advance()
            t = ready.pop(g)
            assert t.key == key, (t.key, key)
            return t

        def give(t, e):
            sub_free[t.slot] = [e]

        def three(out, w, k, cols, a_h, a_l, start, stop, tok=False):
            H, L = w.hi[:, k, cols], w.lo[:, k, cols]
            if tok:
                return [(out, a_h, L, start, False), (out, a_l, H, False, False), (out, a_h, H, False, stop)]
            return [(out, L, a_h, start, False), (out, H, a_l, False, False), (out, H, a_h, False, stop)]

        C128 = slice(0, 128)

        begun = []

        def begin(key, ah, al, ev_k):
            ws, bs = [take(key, SUBS - 1), take(key, SUBS - 2)], [bank(), bank()]
            es = [None, None]
            for k in range(8):
                for i in range(2):
                    pe.wait(ws[i].ev, bs[i].free)
                    es[i] = pe.mms(three(bs[i].ap[:, :], ws[i], k, C128, ah[:, k, :], al[:, k, :], k == 0, k == 7),
                                   ev_k[k])
            for i in range(2):
                give(ws[i], es[i])
                begun.append((bs[i], es[i]))

        def product(key, ah, al, ev_k):
            return begun.pop(0) if begun else another(key, ah, al, ev_k)

        def another(key, ah, al, ev_k):
            w, b = take(key), bank()
            pe.wait(w.ev, b.free)
            for k in range(w.kt):
                e = pe.mms(three(b.ap[:, :], w, k, C128, ah[:, k, :], al[:, k, :], k == 0, k == w.kt - 1), ev_k[k])
            give(w, e)
            return b, e

        def product_tok(key, ah, al, ev_k):
            bs = [bank() for _ in range(4)]
            es = [None] * 4
            for q in range(4):
                w = take(key)
                pe.wait(w.ev, ev_k)
                for t, b in enumerate(bs):
                    pe.wait(b.free)
                    r = slice(128 * t, 128 * t + 128)
                    its = []
                    for j in range(2):
                        k = 2 * q + j
                        its += three(b.ap[:, :], w, j, slice(0, 512), ah[:, k, r], al[:, k, r], k == 0, k == 7, True)
                    es[t] = pe.mms(its)
                give(w, es[3])
            return list(zip(bs, es))

        z0 = pool.set(ident[:, :], 0.0)
        e_id = pool.select(ident[:, :], [[-1, 128]], 0, 1, ALU.not_equal, 1.0, z0)
        e_on = pool.set(ones[:, :], 1.0 / D)
        t0 = pool.set(tri[:, :], 1.0)
        e_tri = pool.select(tri[:, :], [[1, 128]], 0, -1, ALU.is_ge, 0.0, t0)
        t0 = pool.set(neg[:, :], 0.0)
        e_neg = pool.select(neg[:, :], [[-1, 128]], 0, 1, ALU.is_ge, -1e30, t0)
        t0 = pool.set(perm[:, :], 0.0)
        pv = perm[:, :].rearrange("p (a b c) -> p a b c", a=4, b=2)
        t0 = pool.select(pv[:, :, 0, :], [[-32, 4], [-1, 16]], -16, 1, ALU.not_equal, -1.0, t0)
        e_perm = pool.select(pv[:, :, 1, :], [[-32, 4], [-1, 16]], 0, 1, ALU.not_equal, 1.0, t0)
        for n in Z:
            e = pool.set(Z[n][:, :], 0.0)
        e = pool.set(Z["256"][:, 32:33], 1 / 256, e)
        e = pool.set(Z["128"][:, 32:33], 1 / 128, e)
        e = pool.set(Z["k"][:, 32:33], 1 / 32, e)
        for h in range(2):
            e = pool.set(Z["64"][64 * h:64 * h + 64, 32 + h:33 + h], 1 / 64, e)
        for h in range(4):
            e_Z = e = pool.set(Z["32"][32 * h:32 * h + 32, 32 + h:33 + h], 1 / 32, e)
        c_act = small[:, 0:8]
        clam = small[:, 8:12]
        lnlb, ln1lb, onelb, dif = (small[:, 12 + 8 * i:20 + 8 * i] for i in range(4))
        acol = small[:, 44:46]
        dskip = small[:, 46:54]
        invf = small[:, 54:55]
        one = small[:, 55:56]
        mhalf = small[:, 56:60]
        r2 = small[:, 60:64]
        tk = small[:, 68:72]
        rtok = small[:, 64:68]
        t8 = [small[:, 72 + 8 * i:80 + 8 * i] for i in range(6)]
        sm = small[:, 120:160]
        e_mh = pool.set(mhalf, -0.5, e_Z)
        e_mh = pool.set(one, 1.0, e_mh)

        vec_at, rows, zr = {}, [0, 128, 256], []
        V = ar[:, 40, 0:384].rearrange("p (v n) -> p v n", v=3)
        e_v0 = pool.set(ar[:, 40, 0:384], 0.0, e_mh)
        n_vec = [0]

        def vec(name, tile, src=None, n=None, pieces=None):
            r = rows[tile]
            p = r - 128 * tile
            vec_at[name] = r
            for dst, s in pieces or [((p, p + n, 0, 128), src)]:
                if pieces:
                    dst = (p + dst[0], p + dst[1], dst[2], dst[3])
                act.dma(lambda e, d=V[dst[0]:dst[1], tile, dst[2]:dst[3]], s=s: e.dma_start(d, s), s_vec, e_v0)
                n_vec[0] += 16
            rows[tile] += n
            assert rows[tile] <= 128 * (tile + 1)

        def r128(ap, pat, **kw):
            return ap.rearrange(pat, **kw)

        xs_in = ar[:, 0:8, :].rearrange("p (b h) n -> p b (h n)", b=4)
        xin = I['x'][0].rearrange("(b p) d -> p b d", p=128)
        n_x = [0]
        for b in range(4):
            sp_q.dma(lambda e, b=b: e.dma_start(xs_in[:, b, :], xin[:, b, :]), s_x)
        for _ in range(RAW):
            send()
        vec("ffn_norm", 0, r128(I['ffn_norm'], "l s (t p) -> (l s t) p", p=128), 32)
        vec("mix_norm", 0, r128(I['mix_norm'], "l (t p) -> (l t) p", p=128), 16)
        vec("ple_norm", 0, r128(I['ple_norm'], "l (t p) -> (l t) p", p=128), 16)
        vec("final_norm", 0, r128(I['final_norm'], "(t p) -> t p", p=128), 8)
        vec("gla_gate_bias", 0, r128(I['gla_gate_bias'], "o (t p) -> (o t) p", p=128), 2)
        vec("gla_head_norm", 0, I['gla_head_norm'], 1)
        vec("lru_conv_w", 0, r128(I['lru_conv_w'], "o w (t p) -> (o w t) p", p=128), 16)
        for n in ("lru_conv_b", "lru_ba", "lru_bx", "lru_lambda"):
            vec(n, 0, r128(I[n], "o (t p) -> (o t) p", p=128), 4)
        vec("hgrn_lb_logits", 0, r128(I['hgrn_lb_logits'], "l (t p) -> (l t) p", p=128), 16)
        vec("hgrn_head_norm", 0, I['hgrn_head_norm'], 1)
        vec("norm1", 1, r128(I['norm1_w_2'], "l (t p) -> (l t) p", p=128), 16)
        vec("norm2", 1, r128(I['norm2_w_2'], "l (t p) -> (l t) p", p=128), 16)
        vec("b_ada", 1, r128(I['b_ada_2'], "l (t p) -> (l t) p", p=128), 96)
        vec("q_a", 2, r128(I['q_a_norm_w_2'], "l (t p) -> (l t) p", p=128), 4)
        vec("kv_a", 2, I['kv_a_norm_w_2'], 2)
        vec("conv_w", 2, r128(I['conv_w_2'], "l w (t p) -> (l w t) p", p=128), 64)
        vec("conv_b", 2, r128(I['conv_b_2'], "l (t p) -> (l t) p", p=128), 16)
        vec("ssd_norm", 2, r128(I['ssd_norm_w_2'], "l (t p) -> (l t) p", p=128), 8)
        vec("c", 2, r128(I['c_2'], "o (t p) -> (o t) p", p=128), 8)
        for name, key, w in (("q_nope", 'q_nope_norm_w_2', 64), ("q_pe", 'q_pe_norm_w_2', 32),
                             ("k_nope", 'k_nope_norm_w_2', 64), ("k_pe", 'k_pe_norm_w_2', 32)):
            vec(name, 2, n=2, pieces=[((0, 2, c, c + w), I[key]) for c in range(0, 128, w)])
        for name, key in (("dt_bias", 'dt_bias_2'), ("a_log", 'a_log_2'), ("d_skip", 'd_skip_2')):
            vec(name, 2, n=2, pieces=[((0, 2, 32, 40), I[key])])
        e_vec = (s_vec, n_vec[0])
        e_if = misc_dma(invf, I['inv_freq'].rearrange("(p o) -> p o", o=1))

        b = bank()
        e = pe.trs([(b.ap[:, 128 * i:128 * i + 128], V[:, i, :], ident[:, :]) for i in range(3)], e_vec, e_id, e_on, e_mh, e_Z, e_perm, e_tri, e_neg)
        e_VT = dve.copy(VT[:, :], b.ap[:, 0:384], e)
        e_vt_pe = e
        b.rel(e_VT)

        def col(name, i=0):
            return VT[:, vec_at[name] + i:vec_at[name] + i + 1]

        def cols(name, i, n):
            return VT[:, vec_at[name] + i:vec_at[name] + i + n]

        consts_ready = [None]
        e_c = act.f(c_act, cols("c", 0, 8), ACT.Silu, e_VT)
        lam = cols("lru_lambda", 0, 4)
        a0, a1, a2, a3 = (t8[i][:, 0:4] for i in range(4))
        e = act.f(a0, lam, ACT.Abs, e_VT)
        e = act.f(a1, a0, ACT.Exp, e, scale=-1.0)
        e = act.f(a2, a1, ACT.Ln, e, bias=1.0)
        e = dve.stt(a3, lam, 0.0, a2, MIN, SUB, e, e_VT)
        e_lam = dve.ts(clam, a3, 8.0, MUL, e)
        l0, l1 = cols("hgrn_lb_logits", 0, 8), cols("hgrn_lb_logits", 8, 8)
        e = dve.tt(t8[0], l0, l1, MAX, e_lam)
        e0 = dve.tt(t8[1], l0, t8[0], SUB, e)
        e1 = dve.tt(t8[2], l1, t8[0], SUB, e)
        e0 = act.f(t8[1], t8[1], ACT.Exp, e0)
        e1 = act.f(t8[2], t8[2], ACT.Exp, e1)
        e = dve.tt(t8[3], t8[1], t8[2], ADD, e0, e1)
        e = dve.recip(t8[4], t8[3], e)
        e0 = dve.tt(t8[1], t8[1], t8[4], MUL, e)
        e1 = dve.tt(t8[2], t8[2], t8[4], MUL, e)
        e = dve.tt(t8[3], t8[1], t8[2], ADD, e0, e1)
        e = dve.tt(t8[5], t8[3], t8[1], SUB, e)
        e1 = dve.ts(onelb, t8[5], -1.0, MUL, e, s2=1.0, op1=ADD)
        e0 = act.f(lnlb, t8[5], ACT.Ln, e)
        e1 = act.f(ln1lb, onelb, ACT.Ln, e1)
        e_lb = dve.tt(dif, ln1lb, lnlb, SUB, e0, e1)
        e = act.f(acol[32:40, :], cols("a_log", 0, 2)[32:40, :], ACT.Exp, e_VT)
        e_a = dve.ts(acol[32:40, :], acol[32:40, :], -1.0, MUL, e)
        def shares(dst, g, n, *ev):
            r = slice(32 * g, 32 * g + 32)
            return dve.copy(dst[r, 0:8 * n].rearrange("p (c n) -> p c n", n=n),
                            ident[r, 32 * g:32 * g + 8].unsqueeze(2).to_broadcast([32, 8, n]), *ev)

        e_X = shares(ar[:, 39, :], 1, 64, e_VT)
        b = bank()
        e = pe.mms([(b.ap[:, 4 * l + t:4 * l + t + 1],
                     ar[32:40, 39, 128 * t:128 * t + 128], col("d_skip", l)[32:40, :], True, True)
                    for l in range(2) for t in range(4)], e_X, b.free)
        e_X = e
        e_dsk = dve.copy(dskip, b.ap[:, 0:8], e)
        b.rel(e_dsk)
        consts_ready[0] = [e_c, e_lam, e_lb, e_a, e_dsk]

        xe, xrd = [None] * 8, [[] for _ in range(8)]
        st = {"hfree": [], "R": None, "Rrd": [], "sqf": [[], []], "accf": [], "T1f": [[], []], "T3f": [[], []],
              "afree": [e_vt_pe, e_X], "sfree": [], "hk": [None] * 8}

        for t in range(8):
            b = bank()
            e = pe.trs([(b.ap[:, 128 * k:128 * k + 128], xs_in[:, k, 128 * t:128 * t + 128], ident[:, :]) for k in range(4)],
                       (s_x, 64), b.free)
            xe[t] = act.f(x[:, t, :], b.ap[:, :], ACT.Copy, e)
            b.rel(xe[t])
            st["afree"] = [e, e_vt_pe, e_X]

        def square(t):
            if t == 0:
                e = act.f(acc[:, :], x[:, 0, :], ACT.Square, xe[0], st["accf"])
                st["acc"] = e
                return e
            i = t % 2
            e = act.f(sq[i][:, :], x[:, t, :], ACT.Square, xe[t], st["sqf"][i])
            if t == 1:
                st["acc"] = dve.stt(acc[:, :], acc[:, :], EPS * D / 128, sq[i][:, :], ADD, ADD, e, st["acc"])
            else:
                st["acc"] = dve.tt(acc[:, :], acc[:, :], sq[i][:, :], ADD, e, st["acc"])
            st["sqf"][i] = [st["acc"]]
            return e

        def part(t, src, hi, lo, *ev):
            e1 = act.f(hi, src, ACT.Copy, *ev)
            e2 = dve.tt(lo, src, hi.bitcast(F32), SUB, e1, *ev)
            return [e1, e2]

        def norm_tile(t, gname, gi):
            g = col(gname, gi + t)
            e1 = act.f(hh[:, t, :], x[:, t, :], ACT.Copy, xe[t], st["hfree"], scale=g)
            e2 = dve.stt(hl[:, t, :], x[:, t, :], g, hh[:, t, :].bitcast(F32), MUL, SUB, e1)
            e3 = square(t)
            st["hk"][t] = [e1, e2]
            xrd[t] = [e1, e2, e3]

        def token_means(src, *ev):
            b = bank()
            return b, pe.mms([(b.ap[:, k:k + 1], src[:, 128 * k:128 * k + 128], ones[:, 0:1], True, True) for k in range(4)],
                             b.free, *ev)

        def along(dst, v, *ev):
            e = dve.stt(sq[0][:, :].rearrange("p (b n) -> p b n", b=4), ident[:, :].unsqueeze(1).to_broadcast([128, 4, 128]),
                        float(D), v.unsqueeze(2).to_broadcast([128, 4, 128]), MUL, MUL, st["sqf"][0], *ev)
            b = bank()
            e = pe.mms([(b.ap[:, :], ones[:, :], sq[0][:, :], True, True)], e, b.free)
            st["sqf"][0] = [e]
            e = act.f(dst, b.ap[:, :], ACT.Copy, e, *ev)
            b.rel(e)
            return e

        def norm_end(key=None):
            b, e = token_means(acc, st["acc"])
            st["accf"] = [e]
            e = dve.copy(tk, b.ap[:, 0:4], e, st.get("tkf"))
            b.rel(e)
            st["rtok"] = pool.tt(rtok, tk, mhalf, ALU.pow, e, e_mh, st["Rrd"])
            st["tkf"] = [st["rtok"]]
            if key:
                begun.append(another(key, hh, hl, st["hk"]))
            st["R"] = along(R[:, :], rtok, st["rtok"], st["Rrd"])
            st["Rrd"] = [st["R"]]

        def gains(nname, l, sc):
            return dve.stt(G[:, :], mod[:, 48 * l + 8 * sc:48 * l + 8 * sc + 8], 1.0, cols(nname, 8 * l, 8), ADD, MUL,
                           mod_ev[0], st.get("Gf"))

        def modulated(l, sh, rr, e_rr, eG):
            bufs = [T1[0], T1[1], T3[0], T3[1]]
            bf = [st["T1f"][0], st["T1f"][1], st["T3f"][0], st["T3f"][1]]
            off = 48 * l + 8 * sh

            def low(t):
                e2 = dve.stt(hl[:, t, :], bufs[t % 4][:, :], mod[:, off + t:off + t + 1], hh[:, t, :].bitcast(F32), ADD, SUB,
                             st["hk"][t][0])
                st["hk"][t] = bf[t % 4] = [st["hk"][t][0], e2]

            for t in range(8):
                e = dve.stt(bufs[t % 4][:, :], x[:, t, :], G[:, t:t + 1], rr, MUL, MUL, e_rr, eG, bf[t % 4], xe[t])
                st["hk"][t] = [act.f(hh[:, t, :], bufs[t % 4][:, :], ACT.Identity, e, st["hfree"],
                                     bias=mod[:, off + t:off + t + 1])]
                xrd[t] = [e]
                if t:
                    low(t - 1)
            low(7)
            st["T1f"], st["T3f"] = [bf[0], bf[1]], [bf[2], bf[3]]
            st["Gf"] = [e]
            return e

        def after(nxt, t):
            if nxt is None:
                return
            if nxt[0] == "ffn":
                norm_tile(t, "ffn_norm", 16 * nxt[1] + 8 * nxt[2])
            elif nxt[0] in ("mix0", "mix1"):
                norm_tile(t, "mix_norm", 8 * (nxt[0] == "mix1"))
            elif nxt[0] == "ple":
                norm_tile(t, "ple_norm", 8 * nxt[1])
            else:
                xrd[t] = [square(t)]
                if nxt[0] == "final":
                    f = col("final_norm", t)
                    d = T1[1 if t else 0][:, :]
                    e = act.f(d, x[:, t, :], ACT.Square, xe[t], st["T1f"][1 if t else 0], scale=f)
                    xrd[t].append(e)
                    if t:
                        e = dve.tt(T1[0][:, :], T1[0][:, :], d, ADD, e, st["acc2"])
                        st["T1f"][1] = [e]
                    st["acc2"] = e

        def deferred(nxt):
            return nxt is not None and nxt[0] in ("ffn", "mix0", "mix1", "ple")

        def enter(nxt):
            if nxt is None or nxt[0] == "final":
                return
            if deferred(nxt):
                begin(nxt, hh, hl, st["hk"])
                norm_end(nxt)
                return
            split(used[0] + SUBS - 1)
            ada_sums()
            nname, sc, sh = ("norm1", 1, 0) if nxt[0] == "mix2" else ("norm2", 4, 3)
            eG = gains(nname, nxt[1], sc)
            norm_end()
            st["Rrd"] = [modulated(nxt[1], sh, R[:, :], st["R"], eG)]
            begin(nxt, hh, hl, st["hk"])

        def ffn(stage, nxt, scaled, scale, gate):
            key = stage
            wait_a = st["afree"]
            hid = [None] * FT
            for j in range(11):
                g1 = []
                for a in range(2):
                    b, e = product(key, hh, hl, st["hk"])
                    i = a
                    if scaled:
                        e = dve.tt(T1[i][:, :], b.ap[:, :], R[:, :], MUL, e, st["R"], st["T1f"][i])
                        b.rel(e)
                        e = act.f(T1[i][:, :], T1[i][:, :], ACT.Silu, e)
                    else:
                        e = act.f(T1[i][:, :], b.ap[:, :], ACT.Silu, e, st["T1f"][i])
                        b.rel(e)
                    g1.append(e)
                for a in range(2):
                    t = 2 * j + a
                    b, e = product(key, hh, hl, st["hk"])
                    i = a
                    if scaled:
                        e = dve.tt(T3[i][:, :], b.ap[:, :], R[:, :], MUL, e, st["R"], st["T3f"][i])
                        b.rel(e)
                        st["Rrd"] = [e]
                        e = dve.tt(T3[i][:, :], T3[i][:, :], T1[i][:, :], MUL, e, g1[a])
                    else:
                        e = dve.tt(T3[i][:, :], b.ap[:, :], T1[i][:, :], MUL, e, g1[a], st["T3f"][i])
                        b.rel(e)
                    st["T1f"][i] = [e]
                    hid[t] = part(t, T3[i][:, :], uh[:, t, :], ul[:, t, :], e, wait_a)
                    st["T3f"][i] = hid[t]
            st["hfree"] = [(pe.sem, pe.n)]
            for m in range(4):
                bs = [bank(), bank()]
                for k0, kt in ((0, 8), (8, 8), (16, 6)):
                    for a in range(2):
                        w = take(key)
                        pe.wait(w.ev, bs[a].free)
                        for k in range(kt):
                            e = pe.mms(three(bs[a].ap[:, :], w, k, C128, uh[:, k0 + k, :], ul[:, k0 + k, :],
                                             k0 + k == 0, k0 + k == FT - 1), hid[k0 + k])
                        give(w, e)
                        if k0 == 16:
                            t = 2 * m + a
                            xe[t] = dve.stt(x[:, t, :], bs[a].ap[:, :], gate(t) if gate else scale, x[:, t, :], MUL, ADD,
                                            e, xe[t], xrd[t])
                            bs[a].rel(xe[t])
                            after(nxt, t)
            st["afree"] = [(pe.sem, pe.n)]
            enter(nxt)

        def out_product(key, nxt, ev_k, gate=None):
            begin(key, ch, cl, ev_k)
            for t in range(8):
                b, e = product(key, ch, cl, ev_k)
                if gate:
                    xe[t] = dve.stt(x[:, t, :], b.ap[:, :], gate(t), x[:, t, :], MUL, ADD, e, xe[t], xrd[t])
                else:
                    xe[t] = dve.tt(x[:, t, :], b.ap[:, :], x[:, t, :], ADD, e, xe[t], xrd[t])
                b.rel(xe[t])
                after(nxt, t)
            st["afree"] = [(pe.sem, pe.n), (dve.sem, dve.n), (act.sem, act.n)]
            enter(nxt)

        def ple(stage, nxt):
            l = stage[1]
            praw = ar[:, 40:42, :].rearrange("p a n -> p (a n)").rearrange("p (b c) -> p b c", b=4)
            e_p = misc_dma(praw, I['p'][l, 0].rearrange("(b p) c -> p b c", p=128), st["afree"])
            pe_ev = []
            for k in range(8):
                b, e = product(stage, hh, hl, st["hk"])
                e = dve.tt(T1[k % 2][:, :], b.ap[:, :], R[:, :], MUL, e, st["R"], st["T1f"][k % 2])
                b.rel(e)
                st["Rrd"] = [e]
                e = act.f(A(16 + k), T1[k % 2][:, :], ACT.Sigmoid, e, st["afree"])
                st["T1f"][k % 2] = [e]
                pe_ev.append(e)
                if k == 3:
                    ek = []
                    for c in range(2):
                        b = bank()
                        e = pe.trs([(b.ap[:, 128 * j:128 * j + 128], praw[:, j, 128 * c:128 * c + 128], ident[:, :])
                                    for j in range(4)], e_p, b.free)
                        ek.append(part(c, b.ap[:, :], ch[:, c, :], cl[:, c, :], e, st["afree"]))
                        b.rel(ek[-1])
            st["hfree"] = [(pe.sem, pe.n)]
            for h in range(2):
                w = take(stage)
                for j in range(4):
                    t = 4 * h + j
                    b = bank()
                    its = []
                    for k in range(2):
                        its += three(b.ap[:, :], w, k, slice(128 * j, 128 * j + 128), ch[:, k, :], cl[:, k, :], k == 0, k == 1)
                    e = pe.mms(its, w.ev, b.free, ek)
                    give(w, e)
                    i = t % 2
                    e = dve.tt(T3[i][:, :], b.ap[:, :], A(16 + t), MUL, e, pe_ev[t], st["T3f"][i])
                    b.rel(e)
                    xe[t] = dve.tt(x[:, t, :], x[:, t, :], T3[i][:, :], ADD, e, xe[t], xrd[t])
                    st["T3f"][i] = [xe[t]]
                    after(nxt, t)
            st["afree"] = [(pe.sem, pe.n), (dve.sem, dve.n), (act.sem, act.n)]
            enter(nxt)

        def final(nxt):
            norm_end()
            f = cols("final_norm", 0, 8)
            if nxt:
                split(used[0] + SUBS - 1)
                ada_sums()
                eG = gains("norm1", nxt[1], 1)
                eG = dve.tt(G[:, :], G[:, :], f, MUL, eG)
                b, e = token_means(T1[0], st["acc2"])
                st["T1f"][0] = [e]
                e1 = dve.tt(r2, rtok, rtok, MUL, st["rtok"], st.get("r2f"))
                e1 = dve.tt(r2, r2, b.ap[:, 0:4], MUL, e1, e)
                b.rel(e1)
                e1 = dve.ts(r2, r2, EPS, ADD, e1)
                e1 = pool.tt(r2, r2, mhalf, ALU.pow, e1)
                e1 = dve.tt(r2, r2, rtok, MUL, e1)
                e1 = along(sq[1][:, :], r2, e1, st["sqf"][1])
                st["r2f"] = [e1]
                st["sqf"][1] = [modulated(nxt[1], 0, sq[1][:, :], e1, eG)]
            for t in range(8):
                xe[t] = dve.stt(x[:, t, :], x[:, t, :], f[:, t:t + 1], R[:, :], MUL, MUL, st["R"], xe[t], xrd[t])
            st["Rrd"] = [xe[7]]
            if nxt:
                begin(nxt, hh, hl, st["hk"])

        def conv(dst, src, w, b, *ev):
            e = dve.ts(dst, src, w(3), MUL, *ev, s2=b, op1=ADD)
            for s in range(1, 4):
                e = dve.stt(dst[:, s:S], src[:, 0:S - s], w(3 - s), dst[:, s:S], MUL, ADD, e)
            return e

        def row_stats(b, n, e):
            rr = sq[1]
            e1 = dve.ts(rr[0:n, :], b.ap[0:n, :], EPS, ADD, e, st["sqf"][1])
            b.rel(e1)
            e1 = act.f(rr[0:n, :], rr[0:n, :], ACT.Sqrt, e1)
            e1 = dve.recip(rr[0:n, :], rr[0:n, :], e1)
            st["sqf"][1] = [e1]
            return rr, e1

        def spread(rr, g, h, n, e, X=None):
            b = bank()
            l = ident[32 * g:32 * g + 32, 32 * g + h:32 * g + h + 1].to_broadcast([32, 128])
            if n > 1:
                l = X[32 * g:32 * g + 32, 128 // n * h:128 // n * h + 128]
            e = pe.mms([(b.ap[:, :], l, rr[32 * g:32 * g + 32, :], True, True)], e, b.free)
            st["sqf"][1] = [e]
            return b, e

        def chunk_mask(dst, n, *ev):
            e = pool.set(dst, 1.0, *ev)
            return pool.set(dst.rearrange("p (c n) -> p c n", n=n)[:, :, 0:1], 0.0, e)

        def mix0(stage, nxt):
            fr = st["afree"]
            hk = st["hk"]
            wbd = ar[:, 42:44, :].rearrange("p a (t n) -> p a t n", n=128)
            up = ar[0:16, 12, 0:256]
            e_z = pool.set(ar[:, 42:44, :], 0.0, fr)
            for a, n in enumerate(('lru_wa', 'lru_wx')):
                for h in range(2):
                    e_w = misc_dma(wbd[64 * h:64 * h + 64, a, :, 64 * h:64 * h + 64],
                                   I[n][0].rearrange("(t h) i j -> h i t j", h=2)[h], e_z)
            e_w = misc_dma(up, I['gla_gate_up'][0], fr)
            cm = A(13)
            e_cm = chunk_mask(cm, 64, fr)
            b, e = product(stage, hh, hl, hk)
            lrT = ar[0:16, 14, :]
            e_lr = dve.tt(lrT, b.ap[0:16, :], R[0:16, :], MUL, e, st["R"], fr)
            b.rel(e_lr)
            ek = []
            for j in range(2):
                b, e = product(stage, hh, hl, hk)
                e = dve.tt(A(18 + j), b.ap[:, :], R[:, :], MUL, e, fr)
                b.rel(e)
                ek.append(e)
            Gc = sm[:, 0:16].rearrange("p (j c) -> p j c", j=2)
            kdt = A(8, 2).rearrange("p a n -> p (a n)").rearrange("p (b n) -> p b n", b=4)
            sts = ar[:, 0:8, :]
            e_g, kt_ev = [], []

            def decay():
                c2, w2 = A(16, 2), A(0, 2)
                e2 = []
                for j in range(2):
                    b = bank()
                    e = pe.mms([(b.ap[:, :], up[:, 128 * j:128 * j + 128], lrT, True, True)], e_lr, e_w, b.free)
                    bi = col("gla_gate_bias", j)
                    e1 = act.f(A(j), b.ap[:, :], ACT.Abs, e, fr, bias=bi)
                    e2.append(dve.ts(A(16 + j), b.ap[:, :], bi, ADD, e1, fr, s2=0.0, op1=MIN))
                    b.rel(e2[j])
                yield 1
                e1 = act.f(w2, w2, ACT.Exp, e1, scale=-1.0)
                e1 = act.f(w2, w2, ACT.Ln, e1, bias=1.0)
                yield 1
                e = dve.tt(w2, c2, w2, SUB, e1, e2)
                for j in range(2):
                    e = dve.scan(A(16 + j), cm, A(j), e, e_cm)
                yield 1
                for j in range(2):
                    cv = A(16 + j).rearrange("p (c n) -> p c n", n=64)
                    e1 = dve.tt(A(j).rearrange("p (c n) -> p c n", n=64), cv[:, :, 63:64].to_broadcast([128, 8, 64]), cv, SUB, e)
                for j in range(2):
                    e_g.append(act.f(Gc[:, j, :], A(16 + j).rearrange("p (c n) -> p c n", n=64)[:, :, 63], ACT.Exp, e,
                                     st.get("smf"), scale=1 / 16))
                yield 1
                e1 = act.f(w2, w2, ACT.Exp, e1, scale=1 / 16)
                yield 1
                e = dve.tt(A(18, 2), A(18, 2), w2, MUL, e1, ek)
                yield 1
                for t in range(2):
                    b = bank()
                    e1 = pe.trs([(b.ap[:, 128 * k:128 * k + 128], A(18 + t)[:, 128 * k:128 * k + 128], ident[:, :])
                                 for k in range(4)], e, b.free)
                    e1 = act.f(kdt[:, :, 128 * t:128 * t + 128], b.ap[:, :].rearrange("p (b n) -> p b n", b=4), ACT.Copy, e1, fr)
                    b.rel(e1)
                    kt_ev.append(e1)

            dec = beside(decay())
            exc = []
            for t in range(4):
                b, e = product(stage, hh, hl, hk)
                e = dve.tt(A(30 + t), b.ap[:, :], R[:, :], MUL, e, fr)
                b.rel(e)
                exc.append(conv(A(34 + t), A(30 + t), lambda j: col("lru_conv_w", 4 * j + t), col("lru_conv_b", t), e, fr))
            bufs, bk = [T1[0], T1[1], T3[0], T3[1]], ["T1f", "T1f", "T3f", "T3f"]
            e_h = [None] * 4

            def lru():
                gi, ga = [10, 11, 15, 14], [12, 13, 16, 17]
                er, ei = [], []
                for a, lst in enumerate((er, ei)):
                    for t in range(4):
                        b = bank()
                        e = pe.mms([(b.ap[:, :], wbd[:, a, t, :], A(34 + t), True, True)], exc[t], e_w, b.free)
                        lst.append(act.f(A((30 + t, gi[t])[a]), b.ap[:, :], ACT.Sigmoid, e, exc[t], fr, e_lr,
                                         bias=col(("lru_ba", "lru_bx")[a], t)))
                        b.rel(lst[t])
                        if t % 2:
                            yield 1
                while dec in side:
                    yield 1
                ea, et = [], []
                for t in range(4):
                    ea.append(act.f(A(ga[t]), A(30 + t), ACT.Exp, er[t], kt_ev, e_g, clam_ev, scale=clam[:, t:t + 1]))
                for t in range(4):
                    et.append(act.f(A(30 + t), A(30 + t), ACT.Tanh, er[t], ea[t], scale=clam[:, t:t + 1]))
                yield 1
                e2 = []
                for t in range(4):
                    e2.append(act.f(bufs[t][:, :], A(ga[t]), ACT.Square, ea[t], st[bk[t]][t % 2]))
                e3 = [dve.tt(A(gi[t]), A(gi[t]), A(34 + t), MUL, ei[t], exc[t]) for t in range(4)]
                yield 1
                for t in range(4):
                    e = dve.stt(A(30 + t), bufs[t][:, :], 1.0, A(30 + t), ADD, MUL, e2[t], et[t])
                    st[bk[t]][t % 2] = [e]
                yield 1
                e = act.f(A(30, 4), A(30, 4), ACT.Sqrt, e, scale=-1.0)
                yield 1
                for t in range(4):
                    e1 = dve.tt(A(gi[t]), A(gi[t]), A(30 + t), MUL, e, e3[t])
                    e_h[t] = dve.scan(A(34 + t), A(ga[t]), A(gi[t]), e1, ea[t])

            clam_ev = e_lam
            rec = beside(lru())
            eq = []
            for j in range(2):
                b, e = product(stage, hh, hl, hk)
                e = dve.stt(A(20 + j), b.ap[:, :], 0.125, R[:, :], MUL, MUL, e, fr)
                b.rel(e)
                eq.append(e)
            vt = A(22, 4)
            for t, (b, e) in enumerate(product_tok(stage, hh, hl, hk)):
                ev = dve.ts(vt[:, t, :], b.ap[:, :], rtok[:, t:t + 1], MUL, e, fr, st["rtok"])
                b.rel(ev)
            eg, exg = [None] * 4, [None] * 4
            e_cat = [None] * 8

            def glas():
                es = None
                while len(kt_ev) < 2:
                    yield 1
                for c in range(8):
                    b = bank()
                    h = 64 * (c % 2)
                    e = pe.mms([(b.ap[:, 256 * j:256 * j + 256], kdt[h:h + 64, c // 2, 128 * j:128 * j + 128],
                                 vt[h:h + 64, c // 2, 256 * j:256 * j + 256], True, True) for j in range(2)], kt_ev, ev, b.free)
                    if c == 0:
                        es = dve.copy(sts[:, 0, :], b.ap[:, :], e, kt_ev)
                    else:
                        p = es
                        for j in range(2):
                            r = slice(256 * j, 256 * j + 256)
                            es = dve.stt(sts[:, c, r], sts[:, c - 1, r], Gc[:, j, c:c + 1], b.ap[:, r], MUL, ADD, e, p, e_g[j])
                    b.rel(es)
                    if c % 2:
                        yield 1
                e_v = e
                so = [A(22 + h) for h in range(4)]
                eo, e2 = [], []
                bs = bank()
                for h in range(5):
                    if h < 4:
                        b = bank()
                        j, r = h // 2, 64 * (h % 2)
                        e = pe.mms([(b.ap[:, 64 * c:64 * c + 64],
                                     sts[r:r + 64, c, 256 * j + 128 * (h % 2):256 * j + 128 * (h % 2) + 128],
                                     A(20 + j)[r:r + 64, 64 * c:64 * c + 64], True, True) for c in range(8)], es, eq, b.free)
                        eo.append(dve.copy(so[h], b.ap[:, :], e, e_v))
                        b.rel(eo[h])
                        e2.append(act.f(bufs[h][:, :], so[h], ACT.Square, eo[h], st[bk[h]][h % 2]))
                    if h:
                        i = h - 1
                        e3 = pe.mms([(bs.ap[0:32, :], Z["128"][:, 32 - i:64 - i], bufs[i][:, :], i == 0, i == 3)], e2[i], bs.free)
                        st[bk[i]][i % 2] = [e3]
                    if h % 2:
                        yield 1
                rr, e_rr = row_stats(bs, 32, e3)
                free = [(pe.sem, pe.n)]
                yield 1
                for h in range(4):
                    b, e = spread(rr, 0, h, 1, e_rr)
                    e = dve.tt(so[h], so[h], b.ap[:, :], MUL, e, eo[h], e2[h])
                    b.rel(e)
                    e = dve.stt(so[h], so[h], col("gla_head_norm"), A(26 + h), MUL, MUL, e, eg[h])
                    e_cat[h] = part(h, so[h], ch[:, h, :], cl[:, h, :], e, free, e_h)
                    if h == 1:
                        yield 1
                for t in range(4):
                    while exg[t] is None:
                        yield 1
                    e = dve.tt(A(38 + t), A(38 + t), A(34 + t), MUL, exg[t], e_h[t])
                    e_cat[4 + t] = part(t, A(38 + t), ch[:, 4 + t, :], cl[:, 4 + t, :], e, free)

            gl = beside(glas())
            for t in range(4):
                b, e = product(stage, hh, hl, hk)
                e = dve.tt(A(26 + t), b.ap[:, :], R[:, :], MUL, e, fr)
                b.rel(e)
                eg[t] = act.f(A(26 + t), A(26 + t), ACT.Silu, e)
            for t in range(4):
                b, e = product(stage, hh, hl, hk)
                e = dve.tt(A(38 + t), b.ap[:, :], R[:, :], MUL, e, fr)
                b.rel(e)
                st["Rrd"] = [e]
                exg[t] = act.f(A(38 + t), A(38 + t), ACT.Gelu_apprx_tanh, e)
            hfree = [(pe.sem, pe.n)]
            finish(rec)
            finish(gl)
            st["hfree"] = hfree
            st["smf"] = [(dve.sem, dve.n)]
            out_product(stage, nxt, e_cat)

        def mix1(stage, nxt):
            fr = st["afree"]
            hk = st["hk"]
            cm = sq[1][:, :]
            e_cm = chunk_mask(cm, 64, st["sqf"][1])
            Gc = ar[:, 43, 0:64].rearrange("p (h c) -> p h c", h=8)
            kdt = ar[:, 0:8, :].rearrange("p a n -> p (a n)").rearrange("p (b n) -> p b n", b=4)
            it = ar[:, 32:40, :].rearrange("p a n -> p (a n)").rearrange("p (b n) -> p b n", b=4)
            e_z, e_kd, e_g = [None] * 8, [None] * 8, [None] * 8

            def decay(g):
                ts = range(4 * g, 4 * g + 4)
                z4, kd4, w4 = A(16 + 4 * g, 4), A(24 + 4 * g, 4), A(8 + 4 * g, 4)
                e_k = act.f(kd4, z4, ACT.Sigmoid, [e_z[t] for t in ts], fr, scale=-1.0)
                yield 1
                e = act.f(w4, z4, ACT.Abs, [e_z[t] for t in ts], fr)
                yield 1
                e = act.f(w4, w4, ACT.Exp, e, scale=-1.0)
                yield 1
                e = act.f(w4, w4, ACT.Ln, e, bias=1.0)
                yield 1
                e_L = dve.stt(z4, z4, 0.0, w4, MIN, SUB, e, e_k)
                yield 1
                e = [act.f(A(8 + t), A(16 + t), ACT.Abs, e_L, bias=dif[:, t:t + 1]) for t in ts]
                yield 1
                e = act.f(w4, w4, ACT.Exp, e, scale=-1.0)
                for t in ts:
                    e_m = dve.ts(A(16 + t), A(16 + t), ln1lb[:, t:t + 1], ADD, e, s2=lnlb[:, t:t + 1], op1=MAX)
                yield 1
                e = act.f(w4, w4, ACT.Ln, e, bias=1.0)
                yield 1
                e = dve.tt(w4, z4, w4, ADD, e_m, e)
                for t in ts:
                    es = dve.scan(A(16 + t), cm, A(8 + t), e, e_cm)
                yield 1
                for t in ts:
                    cv = A(16 + t).rearrange("p (c n) -> p c n", n=64)
                    e1 = dve.tt(A(8 + t).rearrange("p (c n) -> p c n", n=64), cv[:, :, 63:64].to_broadcast([128, 8, 64]),
                                cv, SUB, es)
                for t in ts:
                    e_g[t] = act.f(Gc[:, t, :], A(16 + t).rearrange("p (c n) -> p c n", n=64)[:, :, 63], ACT.Exp, es, fr)
                yield 1
                e1 = act.f(w4, w4, ACT.Exp, e1)
                yield 1
                for t in ts:
                    e_kd[t] = dve.stt(A(24 + t), A(24 + t), onelb[:, t:t + 1], A(8 + t), MUL, MUL, e1, e_k)
                st["sqf"][1] = [e_kd[t]]

            dec = []
            for t in range(8):
                b, e = product(stage, hh, hl, hk)
                e_z[t] = dve.tt(A(16 + t), b.ap[:, :], R[:, :], MUL, e, st["R"], fr)
                b.rel(e_z[t])
                if t % 4 == 3:
                    dec.append(beside(decay(t // 4)))
            for s in range(2):
                for t, (b, e) in enumerate(product_tok(stage, hh, hl, hk)):
                    e_i = dve.ts(it[:, t, 512 * s:512 * s + 512], b.ap[:, :], rtok[:, t:t + 1], MUL, e, fr, st["rtok"])
                    b.rel(e_i)
            e_q, e_kt = [], []
            for t in range(8):
                b, e = product(stage, hh, hl, hk)
                finish(dec[t // 4])
                e = dve.tt(A(16 + t), b.ap[:, :], R[:, :], MUL, e, e_kd[t], e_g[t])
                b.rel(e)
                e_q.append(act.f(A(16 + t), A(16 + t), ACT.Silu, e))
                b = bank()
                e = pe.trs([(b.ap[:, 128 * k:128 * k + 128], A(24 + t)[:, 128 * k:128 * k + 128], ident[:, :])
                            for k in range(4)], e_kd[t], b.free)
                e = dve.copy(kdt[:, :, 128 * t:128 * t + 128], b.ap[:, :].rearrange("p (b n) -> p b n", b=4), e, fr)
                b.rel(e)
                e_kt.append(e)
                e_tr = (pe.sem, pe.n)
            o_rd = [[], []]
            stt_buf = [[A(40), A(41)], [A(42), acc2]]
            e_gs, e_o8 = [None] * 8, [None] * 8
            e_cat = [None] * 8

            def states():
                es = None
                for c in range(9):
                    if c < 8:
                        h0 = 64 * (c % 2)
                        new, old = stt_buf[c % 2], stt_buf[(c + 1) % 2]
                        p, es_c = es, []
                        for q in range(2):
                            b = bank()
                            e = pe.mms([(b.ap[:, 128 * i:128 * i + 128],
                                         kdt[h0:h0 + 64, c // 2, 128 * (4 * q + i):128 * (4 * q + i) + 128],
                                         it[h0:h0 + 64, c // 2, 128 * (4 * q + i):128 * (4 * q + i) + 128], True, True)
                                        for i in range(4)], e_kt, e_i, b.free)
                            if c == 0:
                                e1 = dve.copy(new[q][:, :], b.ap[:, :], e, fr, st["T3f"][0])
                            else:
                                for i in range(4):
                                    r = slice(128 * i, 128 * i + 128)
                                    e1 = dve.stt(new[q][:, r], old[q][:, r], Gc[:, 4 * q + i, c:c + 1], b.ap[:, r], MUL, ADD,
                                                 e, p, e_g, o_rd[c % 2])
                            b.rel(e1)
                            es_c.append(e1)
                    if c:
                        d = c - 1
                        st_d = stt_buf[d % 2]
                        b = bank()
                        e = pe.mms([(b.ap[:, 64 * h:64 * h + 64], st_d[h // 4][:, 128 * (h % 4):128 * (h % 4) + 128],
                                     A(16 + h)[:, 64 * d:64 * d + 64], True, True) for h in range(8)], es, e_q, b.free)
                        o_rd[d % 2] = [e]
                        e_o = dve.copy(ar[:, 24:32, 64 * d:64 * d + 64], b.ap[:, :].rearrange("p (h n) -> p h n", h=8), e, e_tr)
                        b.rel(e_o)
                    if c < 8:
                        es = es_c
                    if c % 2:
                        yield 1
                st["T3f"][0] = [e]
                free = [e]
                bs = bank()
                tmp = [T1[0], T1[1], T3[1]]
                tf = [st["T1f"][0], st["T1f"][1], st["T3f"][1]]
                e2s = [None] * 8
                for h in range(11):
                    if h > 2:
                        i = h - 3
                        e3 = pe.mms([(bs.ap[0:32, :], Z["128"][:, 32 - i:64 - i], tmp[i % 3][:, :], i == 0, i == 7)], e2s[i], bs.free)
                        tf[i % 3] = [e3]
                    if h < 8:
                        e2s[h] = act.f(tmp[h % 3][:, :], A(24 + h), ACT.Square, e_o, tf[h % 3])
                    if h == 5:
                        yield 1
                st["T1f"], st["T3f"][1] = [tf[0], tf[1]], tf[2]
                rr, e_rr = row_stats(bs, 32, e3)
                yield 1
                for h in range(8):
                    b, e = spread(rr, 0, h, 1, e_rr)
                    e = dve.tt(A(24 + h), A(24 + h), b.ap[:, :], MUL, e, e_o, e2s[h])
                    b.rel(e)
                    while e_gs[h] is None:
                        yield 1
                    e = dve.stt(A(24 + h), A(24 + h), col("hgrn_head_norm"), A(8 + h), MUL, MUL, e, e_gs[h])
                    e_cat[h] = part(h, A(24 + h), ch[:, h, :], cl[:, h, :], e, free)
                    if h % 4 == 3:
                        yield 1

            sts = beside(states())
            for t in range(8):
                b, e = product(stage, hh, hl, hk)
                e = dve.tt(A(8 + t), b.ap[:, :], R[:, :], MUL, e, e_kd[t])
                b.rel(e)
                st["Rrd"] = [e]
                e_gs[t] = act.f(A(8 + t), A(8 + t), ACT.Silu, e)
            hfree = [(pe.sem, pe.n)]
            finish(sts)
            st["hfree"] = hfree
            out_product(stage, nxt, e_cat)

        acc2 = T3[0][:, :]

        def mix2(stage, nxt):
            l = stage[1]
            fr = st["afree"]
            hk = st["hk"]
            tok4 = "p (b n) -> p b n"
            co, si, an, tu = A(6), A(7), A(14), A(15)
            pos = tu.bitcast(I32)
            e = misc_dma(pos, I['positions_2'].to_broadcast([128, S]), fr)
            e = dve.copy(an, pos, e, fr)
            e = dve.ts(an, an, invf, MUL, e, e_if)
            MAGIC = 1.5 * 2.0 ** 23
            e1 = dve.ts(tu, an, 1 / (2 * np.pi), MUL, e, s2=MAGIC, op1=ADD)
            e1 = dve.ts(tu, tu, MAGIC, SUB, e1)
            c1 = 6.28125
            c2 = 2029 / 2.0 ** 20
            c3 = float(np.float32(2 * np.pi - c1 - c2))
            for cc in (c1, c2, c3):
                e1 = dve.stt(an, tu, -cc, an, MUL, ADD, e1)
            e1 = dve.ts(an, an, float(np.float32(3.1415925)), MIN, e1, s2=-float(np.float32(3.1415925)), op1=MAX)
            e_si = act.f(si, an, ACT.Sin, e1, fr)
            e = act.f(co, an, ACT.Sin, e1, fr, scale=0.5)
            e = act.f(co, co, ACT.Square, e)
            e_co = dve.ts(co, co, -2.0, MUL, e, s2=1.0, op1=ADD)
            cm = sq[0][:, :]
            X2, X4, two = A(11), A(3)[:, 0:256], A(3)[:, 256:512]
            for g in range(3):
                e_X = shares(X2, g, 64, fr)
            e_X = shares(X4, 1, 32, fr)
            for i, m in enumerate((ident, perm)):
                e_X = dve.copy(two[0:32, 128 * i:128 * i + 128].rearrange("p (a n) -> p a n", a=4),
                               m[0:32, 0:32].unsqueeze(1).to_broadcast([32, 4, 32]), fr)
            KP, QA, KA = A(38), [A(4), A(5)], A(12)
            bs = bank()
            b, e = product(stage, hh, hl, hk)
            e_kp = dve.copy(KP[0:32, :], b.ap[0:32, :], e, fr)
            e2 = act.f(T1[0][0:32, :], KP[0:32, :], ACT.Square, e_kp, st["T1f"][0])
            e2k = e2
            dt, ad, w8 = A(13), A(43), T3[0]
            bi = col("dt_bias", l)[32:40, :]
            e3 = act.f(w8[32:40, :], b.ap[32:40, :], ACT.Abs, e_kp, st["T3f"][0], bias=bi)
            e4 = dve.ts(dt[32:40, :], b.ap[32:40, :], bi, ADD, e3, fr, s2=0.0, op1=MAX)
            b.rel(e4)
            e3 = act.f(w8[32:40, :], w8[32:40, :], ACT.Exp, e3, scale=-1.0)
            e3 = act.f(w8[32:40, :], w8[32:40, :], ACT.Ln, e3, bias=1.0)
            e_dt = dve.tt(dt[32:40, :], dt[32:40, :], w8[32:40, :], ADD, e3, e4)
            st["T3f"][0] = [e_dt]
            e_cm = chunk_mask(cm, 128, st["sqf"][0])
            e = dve.ts(w8[32:40, :], dt[32:40, :], acol[32:40, l:l + 1], MUL, e_dt)
            e_ad = dve.scan(ad[32:40, :], cm[32:40, :], w8[32:40, :], e, e_cm, fr)
            st["T3f"][0] = [e_ad]
            st["sqf"][0] = [e_ad]
            e3 = pe.mms([(bs.ap[0:32, :], Z["k"][0:32, 30:62], T1[0][0:32, :], True, False)], e2, bs.free)
            st["T1f"][0] = [e3]
            e_qa = []
            for j in range(3):
                b, e = product(stage, hh, hl, hk)
                d = QA[j] if j < 2 else KA
                e1 = dve.copy(d, b.ap[:, :], e, fr)
                i = (j + 1) % 2
                b.rel(e1)
                e2 = act.f(T1[i][:, :], d, ACT.Square, e1, st["T1f"][i])
                zz = Z["256"][:, 32:64] if j < 2 else Z["128"][:, 31:63]
                e3 = pe.mms([(bs.ap[0:32, :], zz, T1[i][:, :], False, j == 2)], e2)
                st["T1f"][i] = [e3]
                e_qa.append([e1, e2])
            rr, e_rr = row_stats(bs, 32, e3)
            e_xb = []

            def convolved(t):
                b, e = product(stage, hh, hl, hk)
                i = t % 2
                e = act.f(T3[i][:, :], b.ap[:, :], ACT.Copy, e, st["T3f"][i])
                b.rel(e)
                e1 = conv(A(16 + t), T3[i][:, :], lambda j: col("conv_w", 32 * l + 8 * j + t), col("conv_b", 8 * l + t), e, fr)
                st["T3f"][i] = [e1]
                e_xb.append(act.f(A(16 + t), A(16 + t), ACT.Silu, e1))

            for t in range(4):
                convolved(t)
                if t == 1:
                    e_n = []
                    for j in range(3):
                        b, e = spread(rr, 0, 0 if j < 2 else 1, 1, e_rr)
                        d = QA[j] if j < 2 else KA
                        wc = col("q_a", 2 * l + j) if j < 2 else col("kv_a", l)
                        e = dve.stt(d, d, wc, b.ap[:, :], MUL, MUL, e, e_qa[j])
                        b.rel(e)
                        e_n.append(part(j, d, ch[:, j, :], cl[:, j, :], e, fr))
                    b, e = spread(rr, 0, 2, 1, e_rr)
                    e = dve.stt(KP[0:32, :], KP[0:32, :], col("k_pe", l)[0:32, :], b.ap[0:32, :], MUL, MUL, e, e_kp, e2k)
                    b.rel(e)
                    e_kp = e
                if t == 3:
                    b1, b2 = bank(), bank()
                    e1 = pe.mms([(b1.ap[:, :], two[0:32, 0:128], KP[0:32, :], True, True),
                                 (b2.ap[:, :], two[0:32, 128:256], KP[0:32, :], True, True)],
                                e_kp, e_X, b1.free, b2.free)
                    e2 = dve.tt(A(14), b1.ap[:, :], co, MUL, e1, e_co)
                    b1.rel(e2)
                    e3 = dve.tt(A(15), b2.ap[:, :], si, MUL, e1, e_si)
                    b2.rel(e3)
                    e_kpe = dve.tt(KP, A(14), A(15), ADD, e2, e3)
            bs = bank()
            QN, QP, KN, vt = [A(28 + j) for j in range(4)], [A(32), A(33)], [A(34 + j) for j in range(4)], A(39, 4)
            e_q = {}
            pend = []

            def means():
                i, src, rows, zz, e2, start, stop = pend.pop(0)
                e3 = pe.mms([(bs.ap[rows:rows + 32, :], zz, T1[i][:, :], start, stop)], e2, bs.free)
                st["T1f"][i] = [e3]
                return e3

            def stat(rows, zz, src, e, start, stop):
                i = stat.n % 2
                stat.n += 1
                if pend:
                    means()
                e2 = act.f(T1[i][:, :], src, ACT.Square, e, st["T1f"][i])
                pend.append((i, src, rows, zz, e2, start, stop))
                return e2

            stat.n = 0
            for s in range(2):
                w = take(stage)
                for m in range(3):
                    b = bank()
                    its = []
                    for k in range(2):
                        its += three(b.ap[:, :], w, k, slice(128 * m, 128 * m + 128), ch[:, k, :], cl[:, k, :], k == 0, k == 1)
                    e = pe.mms(its, w.ev, b.free, e_n[0], e_n[1])
                    give(w, e)
                    d = QN[2 * s + m] if m < 2 else QP[s]
                    e1 = dve.copy(d, b.ap[:, :], e, fr)
                    e2 = stat(0 if m < 2 else 32,
                                  Z["64"][:, 32 - 2 * (2 * s + m):64 - 2 * (2 * s + m)] if m < 2 else Z["32"][:, 32 - 4 * s:64 - 4 * s],
                                  d, e1, s == 0 and m != 1, s == 1 and m != 0)
                    b.rel(e1)
                    e_q[(s, m)] = [e1, e2]
            w = take(stage)
            e_kn = []
            for j in range(4):
                b = bank()
                e = pe.mms(three(b.ap[:, :], w, 0, slice(128 * j, 128 * j + 128), ch[:, 2, :], cl[:, 2, :], True, True),
                           w.ev, b.free, e_n[2])
                e1 = dve.copy(KN[j], b.ap[:, :], e, fr)
                e2 = stat(64, Z["64"][:, 32 - 2 * j:64 - 2 * j], KN[j], e1, j == 0, j == 3)
                b.rel(e1)
                e_kn.append([e1, e2])
            for k in range(4):
                b = bank()
                r = slice(128 * k, 128 * k + 128)
                e = pe.mms(three(b.ap[:, :], w, 0, slice(512, 1024), ch[:, 2, r], cl[:, 2, r], True, True, True),
                           w.ev, b.free, e_n[2])
                e_v = act.f(vt[:, k, :], b.ap[:, :], ACT.Copy, e, fr)
                b.rel(e_v)
            give(w, e)
            e_up = e
            e3 = means()
            e_QN, e_QP, e_KN = [], [], []

            def normed():
                rr, e_rr = row_stats(bs, 96, e3)
                yield 1
                for j in range(4):
                    b, e = spread(rr, 0, 2 * j, 2, e_rr, X2)
                    e = dve.stt(QN[j], QN[j], col("q_nope", l), b.ap[:, :], MUL, MUL, e, e_q[(j // 2, j % 2)])
                    b.rel(e)
                    e_QN.append(e)
                    b, e = spread(rr, 2, 2 * j, 2, e_rr, X2)
                    e = dve.stt(KN[j], KN[j], col("k_nope", l), b.ap[:, :], MUL, MUL, e, e_kn[j])
                    b.rel(e)
                    e_KN.append(e)
                    yield 1
                for s in range(2):
                    b, e = spread(rr, 1, 4 * s, 4, e_rr, X4)
                    e = dve.stt(QP[s], QP[s], col("q_pe", l), b.ap[:, :], MUL, MUL, e, e_q[(s, 2)])
                    b.rel(e)
                    yield 1
                    b = bank()
                    e1 = pe.mms([(b.ap[:, :], perm[:, :], QP[s], True, True)], e, b.free)
                    i = s
                    e2 = dve.tt(T3[i][:, :], b.ap[:, :], si, MUL, e1, st["T3f"][i])
                    b.rel(e2)
                    e3_ = dve.tt(QP[s], QP[s], co, MUL, e1)
                    e3_ = dve.tt(QP[s], QP[s], T3[i][:, :], ADD, e2, e3_)
                    st["T3f"][i] = [e3_]
                    e_QP.append(e3_)
                    yield 1

            nrm = beside(normed())
            for t in range(4, 8):
                convolved(t)
            e_zs = []
            for t in range(4):
                b, e = product(stage, hh, hl, hk)
                e_zs.append(act.f(A(24 + t), b.ap[:, :], ACT.Silu, e, fr))
                b.rel(e_zs[-1])
            st["hfree"] = [(pe.sem, pe.n)]
            sfree = [(pe.sem, pe.n)]
            finish(nrm)
            done = [(pe.sem, pe.n), (act.sem, act.n), (dve.sem, dve.n)]
            SC = 96.0 ** -0.5
            flat = sp[:, :, :].rearrange("p a n -> p (a n)")

            def P(i, q):
                o = 1280 * i + 64 * q * (q + 1)
                return flat[:, o:o + 128 * q + 128]

            def PT(i, k):
                o = 2560 + 1280 * i + 512 * k - 64 * k * (k - 1)
                return flat[:, o:o + 512 - 128 * k]

            mx = [t8[0], t8[1]]
            Pf, PTf, mxf = [sfree, sfree], [sfree, sfree], [[], []]
            e_cat = [None] * 8
            heads = {}

            def scores(h):
                i = h % 2
                j, r, g = h // 2, 64 * (h % 2), 32 * (h % 4)
                es = []
                for q in range(4):
                    b = bank()
                    n = 128 * q + 128
                    c = slice(128 * q, n)
                    e = pe.mms([(b.ap[:, 0:n], QN[j][r:r + 64, c], KN[j][r:r + 64, 0:n], True, False),
                                (b.ap[:, 0:n], QP[h // 4][g:g + 32, c], KP[g:g + 32, 0:n], False, False),
                                (b.ap[:, c], ident[:, :], neg[:, :], False, True)], e_QN, e_QP, e_KN, e_kpe, b.free)
                    m = mx[i]
                    e1 = dve.rmax(m[:, q:q + 1], b.ap[:, 0:n], e, mxf[i])
                    e1 = dve.ts(m[:, q:q + 1], m[:, q:q + 1], -SC, MUL, e1)
                    e2 = act.f(P(i, q), b.ap[:, 0:n], ACT.Exp, e1, Pf[i], bias=m[:, q:q + 1], scale=SC,
                               accum_out=m[:, 4 + q:5 + q])
                    b.rel(e2)
                    es.append(e2)
                    advance()
                e1 = dve.recip(m[:, 4:8], m[:, 4:8], es)
                e3 = []
                for q in range(4):
                    e3.append(dve.ts(P(i, q), P(i, q), m[:, 4 + q:5 + q], MUL, e1))
                mxf[i] = [e3[3]]
                heads[h] = e3

            ob = [None]

            def values(h):
                i = h % 2
                e3 = heads[h]
                ep = []
                for k in range(4):
                    b = bank()
                    e = pe.trs([(b.ap[:, 128 * q:128 * q + 128], P(i, q)[:, 128 * k:128 * k + 128], ident[:, :])
                                for q in range(k, 4)], e3, b.free)
                    fn = dve.copy if k % 2 else (lambda o, s, *ev: act.f(o, s, ACT.Copy, *ev))
                    ep.append(fn(PT(i, k), b.ap[:, 128 * k:S], e, PTf[i]))
                    b.rel(ep[-1])
                    if k % 2:
                        advance()
                Pf[i] = [e]
                if h % 2 == 0:
                    ob[0] = bank()
                b = ob[0]
                r = 64 * (h % 2)
                e = pe.mms([(b.ap[r:r + 64, 128 * k:S], vt[:, k, 64 * h:64 * h + 64], PT(i, k), k == 0, k == 3)
                            for k in range(4)], ep, e_v, b.free)
                PTf[i] = [e]
                if h % 2:
                    e_cat[h // 2] = part(h, b.ap[:, :], ch[:, h // 2, :], cl[:, h // 2, :], e, e_up)
                    b.rel(e_cat[h // 2])

            def states():
                X3, TKs, als = T3[0][:, :], T1[0], T1[1]
                e_X = shares(X3, 1, 64, st["T3f"][0])
                b = bank()
                TKt = TKs[:, 0:64].rearrange("p (a b h) -> p a b h", a=2, b=4)
                its = []
                for a, src in enumerate((dt, ad)):
                    for k in range(4):
                        c = 32 * a + 8 * k
                        its.append((b.ap[:, c:c + 8], src[32:40, 128 * k:128 * k + 128], ident[32:40, 32:40]))
                e = pe.trs(its, e_dt, e_ad, b.free)
                e_tk = dve.copy(TKs[:, 0:64], b.ap[:, 0:64], e, st["T1f"][0])
                b.rel(e_tk)
                al = als[:, 0:32].rearrange("p (b h) -> p b h", b=4)
                cd = als[:, 32:64].rearrange("p (b h) -> p b h", b=4)
                de = als[:, 64:96].rearrange("p (b h) -> p b h", b=4)
                b = bank()
                ends = ad[32:40, :].rearrange("p (b n) -> p b n", n=128)[:, :, 127]
                e = pe.mms([(b.ap[:, 4 * h:4 * h + 4], ident[32:40, 32 + h:33 + h].to_broadcast([8, 128]), ends, True, True)
                            for h in range(8)], e_ad, b.free)
                e_al = dve.copy(al, b.ap[:, 0:32].rearrange("p (h b) -> p b h", b=4), e, st["T1f"][1])
                b.rel(e_al)
                yield 1
                e_cd = act.f(cd, al, ACT.Exp, e_al)
                e = dve.tt(de, al, TKt[:, 1], SUB, e_al, e_tk)
                e_de = act.f(de, de, ACT.Exp, e)
                yield 1
                xt = sp[:, 10:14, :]
                xd = [A(i) for i in (4, 5, 6, 7)]
                Bt = [A(12), A(14)]
                PV = [None, A(15), sp[:, 14, :], sp[:, 15, :]]
                e_xt, e_xd, e_bt, e_pv = [], [], [], [None]
                xd4 = A(4, 4)
                for t in range(4):
                    b = bank()
                    e = pe.trs([(b.ap[:, 128 * k:128 * k + 128], A(16 + t)[:, 128 * k:128 * k + 128], ident[:, :])
                                for k in range(4)], e_xb, b.free)
                    o = xt[:, :, 128 * t:128 * t + 128].rearrange("p b (h n) -> p b h n", h=2)
                    e = dve.tt(o, b.ap[:, :].rearrange("p (b h n) -> p b h n", b=4, h=2),
                               TKt[:, 0, :, 2 * t:2 * t + 2].unsqueeze(3).to_broadcast([128, 4, 2, 64]), MUL, e, e_tk, done)
                    b.rel(e)
                    e_xt.append(e)
                    e_xd.append(dve.tt(xd4[:, :, 128 * t:128 * t + 128].rearrange("p b (h n) -> p b h n", h=2), o,
                                       de[:, :, 2 * t:2 * t + 2].unsqueeze(3).to_broadcast([128, 4, 2, 64]), MUL, e, e_de, done))
                    yield 1
                for g in range(2):
                    b = bank()
                    e = pe.trs([(b.ap[:, 128 * k:128 * k + 128], A(20 + g)[:, 128 * k:128 * k + 128], ident[:, :])
                                for k in range(4)], e_xb, b.free)
                    e_bt.append(act.f(Bt[g], b.ap[:, :], ACT.Copy, e, done))
                    b.rel(e_bt[-1])
                    yield 1
                for c in range(3):
                    b = bank()
                    e_sm = e = pe.mms([(b.ap[:, 256 * g:256 * g + 256], Bt[g][:, 128 * c:128 * c + 128],
                                        xd[c][:, 256 * g:256 * g + 256], True, True) for g in range(2)], e_bt, e_xd, b.free)
                    if c == 0:
                        e1 = dve.copy(PV[1], b.ap[:, :], e, done)
                    else:
                        o = PV[c + 1].rearrange("p (h n) -> p h n", h=8)
                        e1 = dve.tt(o, PV[c].rearrange("p (h n) -> p h n", h=8),
                                    cd[:, c, :].unsqueeze(2).to_broadcast([128, 8, 64]), MUL, e_pv[c], e_cd, done)
                        e1 = dve.tt(PV[c + 1], PV[c + 1], b.ap[:, :], ADD, e1, e)
                    b.rel(e1)
                    e_pv.append(e1)
                    yield 1
                Gm = [acc[:, :], sq[0][:, :]]
                gmf = [st["accf"], st["sqf"][0]]
                e_gm = []
                for g in range(2):
                    b = bank()
                    e = pe.mms([(b.ap[:, 128 * k:128 * k + 128], A(20 + g)[:, 128 * k:128 * k + 128],
                                 A(22 + g)[:, 128 * k:128 * k + 128], True, True) for k in range(4)], e_xb, b.free)
                    e = dve.tt(Gm[g].rearrange(tok4, b=4), b.ap[:, :].rearrange(tok4, b=4),
                               tri[:, :].unsqueeze(1).to_broadcast([128, 4, 128]), MUL, e, gmf[g])
                    b.rel(e)
                    e_gm.append(e)
                    yield 1
                W = [d.rearrange(tok4, b=4) for d in xd]
                Wf = [[e_sm] for _ in range(4)]
                e_W = [None] * 8
                E = T3[1][:, :]
                bs = bank()
                e_y, late = [], []
                for t in range(4):
                    for h in (2 * t, 2 * t + 1):
                        b = bank()
                        e = pe.mms([(b.ap[:, :], ident[32:40, 32 + h:33 + h].to_broadcast([8, 128]), ad[32:40, :], True, True)],
                                   e_ad, b.free)
                        bv = b.ap[:, :].rearrange(tok4, b=4)
                        for k in range(4):
                            e1 = dve.ts(W[h % 4][:, k, :], bv[:, k, :], TKt[:, 1, k, h:h + 1], SUB, e, e_tk, Wf[h % 4],
                                        s2=0.0, op1=MIN)
                        b.rel(e1)
                        e1 = act.f(xd[h % 4], xd[h % 4], ACT.Exp, e1)
                        e_W[h] = dve.tt(xd[h % 4], xd[h % 4], Gm[h // 4], MUL, e1, e_gm[h // 4])
                        yield 1
                    b = bank()
                    e = pe.mms([(b.ap[:, :], X3[32:40, 128 * t:128 * t + 128], ad[32:40, :], True, True)], e_ad, e_X, b.free)
                    st["T3f"][0] = [e]
                    e_E = act.f(E, b.ap[:, :], ACT.Exp, e, st["T3f"][1])
                    b.rel(e_E)
                    y = A(16 + t)
                    b = bank()
                    e = pe.mms([(b.ap[64 * h:64 * h + 64, 128 * c:128 * c + 128],
                                 xt[:, c, 128 * t + 64 * h:128 * t + 64 * h + 64],
                                 W[(2 * t + h) % 4][:, c, :], True, True) for c in range(4) for h in range(2)],
                               e_xt, e_W[2 * t], e_W[2 * t + 1], b.free)
                    Wf[(2 * t) % 4] = Wf[(2 * t + 1) % 4] = [e]
                    e = dve.stt(y, y, dskip[:, 4 * l + t:4 * l + t + 1], b.ap[:, :], MUL, ADD, e, e_xb[t], e_xt)
                    b.rel(e)
                    yield 1
                    b = bank()
                    e1 = pe.mms([(b.ap[:, 128 * c:128 * c + 128], PV[c][:, 128 * t:128 * t + 128],
                                  A(22 + t // 2)[:, 128 * c:128 * c + 128], True, True) for c in range(1, 4)], e_pv[3], b.free)
                    e1 = dve.tt(E[:, 128:S], E[:, 128:S], b.ap[:, 128:S], MUL, e1, e_E)
                    b.rel(e1)
                    e = dve.tt(y[:, 128:S], y[:, 128:S], E[:, 128:S], ADD, e, e1)
                    e = dve.tt(y, y, A(24 + t), MUL, e, e_zs[t])
                    yield 1
                    e2 = act.f(E, y, ACT.Square, e, e1)
                    yield 1
                    e3 = pe.mms([(bs.ap[0:32, :], Z["256"][:, 32 - t // 2:64 - t // 2], E, t == 0, t == 3)], e2, bs.free)
                    st["T3f"][1] = [e3]
                    e_y.append([e, e2])
                st["T1f"] = [[(dve.sem, dve.n)], [(dve.sem, dve.n)]]
                st["accf"] = [e_W[3]]
                st["sqf"][0] = [e_W[7]]
                rr, e_rr = row_stats(bs, 32, e3)
                yield 1
                end = [(pe.sem, pe.n)]
                for g in range(2):
                    b, e = spread(rr, 0, g, 1, e_rr)
                    for t in (2 * g, 2 * g + 1):
                        y = A(16 + t)
                        e1 = dve.stt(y, y, col("ssd_norm", 4 * l + t), b.ap[:, :], MUL, MUL, e, e_y[t])
                        e_cat[4 + t] = part(t, y, ch[:, 4 + t, :], cl[:, 4 + t, :], e1, end, e_xd, e_pv)
                    b.rel(e1)

            ssd = beside(states())
            for h in range(9):
                if h < 8:
                    scores(h)
                if h:
                    values(h - 1)
            finish(ssd)
            st["hfree"] = [(pe.sem, pe.n), (dve.sem, dve.n), (act.sem, act.n)]
            out_product(stage, nxt, e_cat, lambda t: mod[:, 48 * l + 16 + t:48 * l + 17 + t])

        def first(stage):
            for t in range(8):
                after(stage, t)
            enter(stage)

        first(stages[0])
        for i, stage in enumerate(stages):
            nxt = stages[i + 1] if i + 1 < len(stages) else None
            if stage[0] == "ffn":
                ffn(stage, nxt, True, 0.5, None)
            elif stage[0] == "ffn2":
                ffn(stage, nxt, False, None, lambda t, l=stage[1]: mod[:, 48 * l + 40 + t:48 * l + 41 + t])
            elif stage[0] == "mix0":
                mix0(stage, nxt)
            elif stage[0] == "mix1":
                mix1(stage, nxt)
            elif stage[0] == "ple":
                ple(stage, nxt)
            elif stage[0] == "final":
                final(nxt)
            elif stage[0] == "mix2":
                mix2(stage, nxt)

        od = out[0].rearrange("(b p) d -> p b d", p=128)
        for k in range(4):
            for h in range(2):
                b = bank()
                e = pe.trs([(b.ap[:, 128 * j:128 * j + 128], x[:, 4 * h + j, 128 * k:128 * k + 128], ident[:, :])
                            for j in range(4)], xe, b.free)
                d = A(2 * k + h)
                e = act.f(d, b.ap[:, :], ACT.Copy, e, st["afree"]) if h else dve.copy(d, b.ap[:, :], e, st["afree"])
                b.rel(e)
                sp_q.dma(lambda q, d=d, k=k, h=h: q.dma_start(od[:, k, 512 * h:512 * h + 512], d), s_out, e)
        sp_q.wait((s_out, 16 * 8), (s_misc, misc[0]))

        block = ctx.enter_context(nc.Block())
        block.sync(lambda e: sp_q.run(e))
        block.scalar(lambda e: act.run(e))
        block.vector(lambda e: dve.run(e))
        block.gpsimd(lambda e: pool.run(e))
        block.tensor(lambda e: pe.run(e))


def kernel(**inputs):
    import concourse.bacc as _bacc
    from concourse.bass_utils import run_bass_kernel_spmd as _run

    inv = np.float32(1.0) / np.power(np.float32(10000.0), np.arange(0, 32, 2, dtype=np.float32) / np.float32(32))
    inputs = dict(inputs, inv_freq=np.tile(inv.astype(np.float32), 8))
    nc = _bacc.Bacc("TRN2", target_bir_lowering=False, num_devices=1)
    arrays, aps = {}, {}
    for name in INS:
        a = np.ascontiguousarray(inputs[name])
        arrays[f"in_{name}"] = a
        aps[name] = nc.dram_tensor(f"in_{name}", a.shape, mybir.dt.from_np(a.dtype), kind="ExternalInput").ap()
    out = nc.dram_tensor("out_0", (1, S, D), F32, kind="ExternalOutput").ap()
    build(nc, aps, out, STAGES)
    r = _run(nc, [arrays], core_ids=[0])
    return r.results[0]["out_0"]
```
